# Optimizing a Trainium2 kernel written in Bass

```python
import math
import jax, jax.numpy as jnp
from jax import lax
import numpy as np

D_MODEL = 1024
BATCH = 1
SEQ = 256
DEPTH = 2

N_MIXERS = 2
N_MEM = 256
HEAD_DIM = 64
MIX_WIDTH = D_MODEL
MEM_HEADS = 4
MEM_WIDTH = MEM_HEADS * HEAD_DIM
TOK_WIDTH = MIX_WIDTH - MEM_WIDTH
DIFF_HEADS = TOK_WIDTH // (2 * HEAD_DIM)
DIFF_V_DIM = 2 * HEAD_DIM
DIFF_WIDTH = DIFF_HEADS * DIFF_V_DIM
QK_A = DIFF_HEADS * 2 * HEAD_DIM
WIN_Q_HEADS = TOK_WIDTH // HEAD_DIM
WIN_GROUP = 3
WIN_KV_HEADS = WIN_Q_HEADS // WIN_GROUP
WIN_Q_WIDTH = WIN_Q_HEADS * HEAD_DIM
WIN_KV_WIDTH = WIN_KV_HEADS * HEAD_DIM
WIN_WIDTH = WIN_Q_WIDTH
WINDOW = 128
BLOCK = 128
D_FF = 2816
A_IN = 2 * QK_A + DIFF_WIDTH + MEM_WIDTH
B_IN = WIN_Q_WIDTH + 2 * WIN_KV_WIDTH + MEM_WIDTH
N_A = (DEPTH + 1) // 2
N_B = DEPTH // 2
DN_ALPHA = (2 * DEPTH) ** 0.25
DN_BETA = (8 * DEPTH) ** -0.25
LN_EPS = 1e-5
NEG = -1e30

kernel_name = 'hybrid_diffattn_swa_gqa_memory_macaron_deepnorm'

def layer_norm(x, g, b):
    xf = x.astype(jnp.float32)
    mu = jnp.mean(xf, -1, keepdims=True)
    var = jnp.mean(jnp.square(xf - mu), -1, keepdims=True)
    return ((xf - mu) * lax.rsqrt(var + LN_EPS) * g.astype(jnp.float32) + b.astype(jnp.float32)).astype(x.dtype)

def swiglu(x, w13, w2):
    gate, up = jnp.split(x @ w13, 2, axis=-1)
    return (jax.nn.silu(gate) * up) @ w2

def alibi_slopes(n):
    return jnp.asarray(2.0 ** (-8.0 * np.arange(1, n + 1) / n), dtype=jnp.float32)

def memory_attention(qm, mem, w_mem_kv):
    b, s, _ = qm.shape
    m = mem.shape[1]
    kv = (mem @ w_mem_kv).reshape(b, m, 2, MEM_HEADS, HEAD_DIM)
    k, v = kv[:, :, 0], kv[:, :, 1]
    q = qm.reshape(b, s, MEM_HEADS, HEAD_DIM)
    sc = jnp.einsum('bshd,bmhd->bhsm', q, k).astype(jnp.float32) * (HEAD_DIM ** -0.5)
    p = jax.nn.softmax(sc, axis=-1).astype(v.dtype)
    return jnp.einsum('bhsm,bmhd->bshd', p, v).reshape(b, s, MEM_WIDTH)

def diff_attention(q, k, v, lam, lam_init, subln_g):
    b, s = q.shape[:2]
    nb = s // BLOCK
    slopes = alibi_slopes(DIFF_HEADS)
    kpos = jnp.arange(s)
    scale = HEAD_DIM ** -0.5
    qb = q.reshape(b, nb, BLOCK, DIFF_HEADS, 2, HEAD_DIM).swapaxes(0, 1)

    def block(args):
        qj, j = args
        sc = jnp.einsum('bqhcd,bkhcd->bhcqk', qj, k).astype(jnp.float32) * scale
        qpos = j * BLOCK + jnp.arange(BLOCK)
        dist = jnp.abs(qpos[:, None] - kpos[None, :]).astype(jnp.float32)
        p = jax.nn.softmax(sc - slopes[:, None, None, None] * dist, axis=-1)
        a = p[:, :, 0] - lam * p[:, :, 1]
        return jnp.einsum('bhqk,bkhe->bqhe', a.astype(v.dtype), v)

    o = lax.map(block, (qb, jnp.arange(nb)))
    of = o.swapaxes(0, 1).reshape(b, s, DIFF_HEADS, DIFF_V_DIM).astype(jnp.float32)
    of = of * lax.rsqrt(jnp.mean(of * of, -1, keepdims=True) + LN_EPS) * subln_g.astype(jnp.float32)
    return (of * (1.0 - lam_init)).astype(v.dtype).reshape(b, s, DIFF_WIDTH)

def window_attention(q, k, v, sink):
    b, s = q.shape[:2]
    nb = s // BLOCK
    scale = HEAD_DIM ** -0.5
    qb = q.reshape(b, nb, BLOCK, WIN_KV_HEADS, WIN_GROUP, HEAD_DIM)

    def band(t):
        tp = jnp.pad(t, ((0, 0), (BLOCK, BLOCK), (0, 0), (0, 0)))
        tp = tp.reshape(b, nb + 2, BLOCK, WIN_KV_HEADS, HEAD_DIM)
        return jnp.concatenate([tp[:, 0:nb], tp[:, 1:nb + 1], tp[:, 2:nb + 2]], axis=2)

    kb, vb = band(k), band(v)
    r = jnp.arange(3 * BLOCK)
    delta = jnp.arange(BLOCK)[:, None] + BLOCK - r[None, :]
    kpos = jnp.arange(nb)[:, None] * BLOCK - BLOCK + r[None, :]
    valid = (jnp.abs(delta) <= WINDOW)[None] & ((kpos >= 0) & (kpos < s))[:, None, :]
    slopes = alibi_slopes(WIN_Q_HEADS).reshape(WIN_KV_HEADS, WIN_GROUP)
    sc = jnp.einsum('bnqkgd,bnrkd->bnkgqr', qb, kb).astype(jnp.float32) * scale
    sc = sc - slopes[:, :, None, None] * jnp.abs(delta).astype(jnp.float32)
    sc = jnp.where(valid[None, :, None, None], sc, NEG)
    sink_l = jnp.broadcast_to(sink.astype(jnp.float32).reshape(1, 1, WIN_KV_HEADS, WIN_GROUP, 1, 1), sc.shape[:-1] + (1,))
    p = jax.nn.softmax(jnp.concatenate([sc, sink_l], axis=-1), axis=-1)[..., :-1]
    o = jnp.einsum('bnkgqr,bnrkd->bnqkgd', p.astype(v.dtype), vb)
    return o.reshape(b, s, WIN_WIDTH)

def mixer_a(x, mem, w_in, w_mem_kv, w_out, lq1, lk1, lq2, lk2, subln_g, layer_idx):
    b, s, _ = x.shape
    h = x @ w_in
    q, k, v, qm = jnp.split(h, [QK_A, 2 * QK_A, 2 * QK_A + DIFF_WIDTH], axis=-1)
    q = q.reshape(b, s, DIFF_HEADS, 2, HEAD_DIM)
    k = k.reshape(b, s, DIFF_HEADS, 2, HEAD_DIM)
    v = v.reshape(b, s, DIFF_HEADS, DIFF_V_DIM)
    lam_init = 0.8 - 0.6 * math.exp(-0.3 * layer_idx)
    f32 = jnp.float32
    lam = (jnp.exp(jnp.sum(lq1.astype(f32) * lk1.astype(f32)))
           - jnp.exp(jnp.sum(lq2.astype(f32) * lk2.astype(f32))) + lam_init)
    o = diff_attention(q, k, v, lam, lam_init, subln_g)
    m = memory_attention(qm, mem, w_mem_kv)
    return jnp.concatenate([o, m], axis=-1) @ w_out

def mixer_b(x, mem, w_in, w_mem_kv, w_out, sink):
    b, s, _ = x.shape
    h = x @ w_in
    q, k, v, qm = jnp.split(h, [WIN_Q_WIDTH, WIN_Q_WIDTH + WIN_KV_WIDTH, WIN_Q_WIDTH + 2 * WIN_KV_WIDTH], axis=-1)
    q = q.reshape(b, s, WIN_Q_HEADS, HEAD_DIM)
    k = k.reshape(b, s, WIN_KV_HEADS, HEAD_DIM)
    v = v.reshape(b, s, WIN_KV_HEADS, HEAD_DIM)
    o = window_attention(q, k, v, sink)
    m = memory_attention(qm, mem, w_mem_kv)
    return jnp.concatenate([o, m], axis=-1) @ w_out

def setup_inputs(seed: int = 0) -> dict:
    key = jax.random.key(seed)
    ks = jax.random.split(key, 24)
    f = jnp.float32

    def nrm(k, shape, scale):
        return jax.random.normal(k, shape, f) * scale

    def gain(k, shape):
        return 1.0 + nrm(k, shape, 0.02)

    a_col = jnp.concatenate([jnp.ones((2 * QK_A,), f), jnp.full((DIFF_WIDTH,), DN_BETA, f), jnp.ones((MEM_WIDTH,), f)])
    b_col = jnp.concatenate([jnp.ones((WIN_Q_WIDTH + WIN_KV_WIDTH,), f), jnp.full((WIN_KV_WIDTH,), DN_BETA, f), jnp.ones((MEM_WIDTH,), f)])
    kv_col = jnp.concatenate([jnp.ones((MEM_WIDTH,), f), jnp.full((MEM_WIDTH,), DN_BETA, f)])
    return {
        'x': nrm(ks[0], (BATCH, SEQ, D_MODEL), 1.0),
        'mem': nrm(ks[1], (BATCH, N_MEM, D_MODEL), 1.0),
        'ffn1_w13': nrm(ks[2], (DEPTH, D_MODEL, 2 * D_FF), D_MODEL ** -0.5),
        'ffn1_w2': nrm(ks[3], (DEPTH, D_FF, D_MODEL), D_FF ** -0.5 * DN_BETA),
        'ln1_g': gain(ks[4], (DEPTH, D_MODEL)),
        'ln1_b': nrm(ks[5], (DEPTH, D_MODEL), 0.02),
        'w_mem_kv': nrm(ks[6], (DEPTH, D_MODEL, 2 * MEM_WIDTH), D_MODEL ** -0.5) * kv_col,
        'w_out': nrm(ks[7], (DEPTH, MIX_WIDTH, D_MODEL), MIX_WIDTH ** -0.5 * DN_BETA),
        'ln2_g': gain(ks[8], (DEPTH, D_MODEL)),
        'ln2_b': nrm(ks[9], (DEPTH, D_MODEL), 0.02),
        'ffn2_w13': nrm(ks[10], (DEPTH, D_MODEL, 2 * D_FF), D_MODEL ** -0.5),
        'ffn2_w2': nrm(ks[11], (DEPTH, D_FF, D_MODEL), D_FF ** -0.5 * DN_BETA),
        'ln3_g': gain(ks[12], (DEPTH, D_MODEL)),
        'ln3_b': nrm(ks[13], (DEPTH, D_MODEL), 0.02),
        'a_w_in': nrm(ks[14], (N_A, D_MODEL, A_IN), D_MODEL ** -0.5) * a_col,
        'a_lambda_q1': nrm(ks[15], (N_A, HEAD_DIM), 0.1),
        'a_lambda_k1': nrm(ks[16], (N_A, HEAD_DIM), 0.1),
        'a_lambda_q2': nrm(ks[17], (N_A, HEAD_DIM), 0.1),
        'a_lambda_k2': nrm(ks[18], (N_A, HEAD_DIM), 0.1),
        'a_subln_g': gain(ks[19], (N_A, DIFF_V_DIM)),
        'b_w_in': nrm(ks[20], (N_B, D_MODEL, B_IN), D_MODEL ** -0.5) * b_col,
        'b_sink': nrm(ks[21], (N_B, WIN_Q_HEADS), 0.5),
    }

def reference(x, mem, ffn1_w13, ffn1_w2, ln1_g, ln1_b, w_mem_kv, w_out, ln2_g, ln2_b,
              ffn2_w13, ffn2_w2, ln3_g, ln3_b, a_w_in, a_lambda_q1, a_lambda_k1,
              a_lambda_q2, a_lambda_k2, a_subln_g, b_w_in, b_sink):
    for i in range(DEPTH):
        x = layer_norm(DN_ALPHA * x + 0.5 * swiglu(x, ffn1_w13[i], ffn1_w2[i]), ln1_g[i], ln1_b[i])
        j = i // N_MIXERS
        if i % N_MIXERS == 0:
            y = mixer_a(x, mem, a_w_in[j], w_mem_kv[i], w_out[i], a_lambda_q1[j], a_lambda_k1[j],
                        a_lambda_q2[j], a_lambda_k2[j], a_subln_g[j], i)
        else:
            y = mixer_b(x, mem, b_w_in[j], w_mem_kv[i], w_out[i], b_sink[j])
        x = layer_norm(DN_ALPHA * x + y, ln2_g[i], ln2_b[i])
        x = layer_norm(DN_ALPHA * x + 0.5 * swiglu(x, ffn2_w13[i], ffn2_w2[i]), ln3_g[i], ln3_b[i])
    return x


_drawn_inputs = setup_inputs


def setup_inputs(seed=0):
    import zlib

    import numpy as np

    out = dict(_drawn_inputs(seed))
    spreads = {}
    factors = {'mem': 4.623,
     'w_mem_kv': 3.79,
     'a_lambda_q1': 3.913,
     'a_lambda_k1': 5.359,
     'a_lambda_q2': 4.175,
     'a_lambda_k2': 8.0,
     'a_subln_g': 8.0,
     'b_sink': 8.0}
    for name, (base, spread) in spreads.items():
        noise = np.random.default_rng([zlib.crc32(name.encode()), seed]).standard_normal(out[name].shape)
        drawn = base * np.exp(spread * noise) if base else spread * noise
        out[name] = __import__('jax').numpy.asarray(drawn.astype(out[name].dtype))
    for name, factor in factors.items():
        out[name] = (out[name] * factor).astype(out[name].dtype)
    return out
```

```python
import math
from contextlib import ExitStack

import concourse.bass as bass
from concourse import mybir

F32 = mybir.dt.float32
F32R = mybir.dt.float32r
ALU = mybir.AluOpType
ACT = mybir.ActivationFunctionType
AX_X = mybir.AxisListType.X

P = 128
RING = 3
UNIT = 2048
HEAD = 64
NEG = -1e30
LN_EPS = 1e-5

DIFF_HEADS = 6
WIN_HEADS = 12
WIN_GROUP = 3
WINDOW = 128
SCORES_PER_SLOT = {"A": 1, "B": 1}
PROBS = 4
LAM_INIT = 0.8 - 0.6 * math.exp(-0.3 * 0)


def slope(n_heads, head):
    return float(2.0 ** (-8.0 * (head + 1) / n_heads))



def head_groups(kind, pair):
    if pair == 3:
        return {0, 1}
    if kind == "A":
        return {2 + 2 * pair, 3 + 2 * pair}
    heads = range(4 * pair, 4 * pair + 4)
    return {2 + g for g in range(6) if set(window_heads(g)) & set(heads)}


def plan_mixer(kind):
    if kind == "A":
        order = ["mem_k", "mem_v", "q_mem", "qk0", "qk1", "v0", "qk2", "qk3", "v1", "qk4", "qk5", "v2"]
        gives = {"q_mem": [0, 1]} | {f"qk{h}": [2 + h] for h in range(6)}
    else:
        order = ["mem_k", "mem_v", "q_mem", "k", "q0", "v", "q1", "q2"]
        gives = {"q_mem": [0, 1]} | {f"q{j}": [2 + 2 * j, 3 + 2 * j] for j in range(3)}
    halves = lambda g: [0] if kind == "A" and g >= 2 else [0, 1]
    order += [3, 0, 1, 2]
    steps, to_score, scored, ready, turned, done = [], [], [], [], [], set()
    to_cat = [3, 0, 1, 2]
    catted = set()
    n_scores = 0

    while order or turned or ready or scored:
        item = order[0] if order else None
        if isinstance(item, str):
            steps.append(("proj", order.pop(0)))
        elif item is not None and n_scores == 8 and item in catted:
            steps.append(("out", order.pop(0)))
        now_values, turned = turned, []
        for g, c in now_values:
            steps.append(("values", g, c))
        if to_cat and head_groups(kind, to_cat[0]) <= done:
            steps.append(("cat", to_cat[0]))
            catted.add(to_cat.pop(0))
        for g in ready:
            for c in halves(g):
                steps.append(("turn", g, c))
                turned.append((g, c))
        ready = scored
        for g in scored:
            steps.append(("probs", g))
        scored = to_score[:SCORES_PER_SLOT[kind]]
        del to_score[:SCORES_PER_SLOT[kind]]
        for g in scored:
            steps.append(("scores", g))
            n_scores += 1
        done |= {g for g, _ in now_values}
        to_score += gives.get(item, [])
    while to_cat:
        steps.append(("cat", to_cat.pop(0)))
    steps += [("out", n) for n in order]
    return steps


FF_CHUNKS = 22


def plan_ffn():
    units = [("w13", 0), ("w13", 1)]
    for s in range(1, FF_CHUNKS // 2):
        units += [("w13", 2 * s), ("w13", 2 * s + 1), ("w2", s - 1)]
    return units + [("w2", FF_CHUNKS // 2 - 1)]


FFN_HEAD = 5
FFN_TURNS = 4


def build(nc, x_in, mem_in, w13_in, w2_in, ln_g, ln_b, w_mem_kv, w_out, a_w_in, lambdas, subln_g,
          b_w_in, b_sink, out):
    depth, dm, ff2 = w13_in[0].shape
    ff = ff2 // 2
    seq = x_in.shape[1]
    KT = dm // P
    TT = seq // P
    assert (KT, TT, ff) == (8, 2, FF_CHUNKS * P) and depth == 2
    alpha = (2 * depth) ** 0.25

    mixers = [plan_mixer("A"), plan_mixer("B")]
    kinds = ["A", "B"]

    units = []
    ffn_first_unit, mixer_unit = {}, {}
    for layer in range(depth):
        for half in range(2):
            ffn_first_unit[layer, half] = len(units)
            units += [(kind, layer, half, n) for kind, n in plan_ffn()]
            if half == 0:
                for step in mixers[layer]:
                    if step[0] in ("proj", "out"):
                        mixer_unit[layer, step] = len(units)
                        units.append((step[0], layer, step[1], 0))
    dmas_of = lambda unit: {"w13": 2, "w2": 1, "out": 1}.get(
        unit[0], 4 if unit[1] == 1 and unit[2] in ("q0", "q1", "q2") else
        2 if unit[1] == 0 and str(unit[2]).startswith("qk") else 1)
    landed_at, total = [], [0] * RING
    for n, unit in enumerate(units):
        total[n % RING] += 16 * dmas_of(unit)
        landed_at.append(total[n % RING])
    n_units = len(units)
    last_unit = [n for n, unit in enumerate(units) if unit[0] == "w2" and unit[3] == FF_CHUNKS // 2 - 1
                 or unit[0] == "out" and unit[2] == 2]

    proj_of, n_proj = {}, 0
    ffn_first_proj, projections, cat_needs = {}, [], {}
    job_of, n_jobs = {}, 0

    def new_job(key):
        nonlocal n_jobs
        job_of[key] = n_jobs
        n_jobs += 1

    for key in [("x", -1, t, h) for t in range(TT) for h in range(2)] + [("mem", t, h) for t in range(TT) for h in range(2)]:
        new_job(key)
    values_count, n_values = {}, 0
    rms_count, n_rms = {}, 0
    scores_count, n_scores = {}, 0
    act_copies, dve_copies = {}, {}
    for layer in range(depth):
        for half in range(2):
            ffn_first_proj[layer, half] = n_proj
            n_proj += FF_CHUNKS
            projections += [("chunk", FF_CHUNKS * (2 * layer + half) + f) for f in range(FF_CHUNKS)]
            norm = 3 * layer + 2 * half
            if norm < 3 * depth - 1:
                for t in range(TT):
                    for h in range(2):
                        new_job(("x", norm, t, h))
            if half == 0:
                for step in mixers[layer]:
                    if step[0] == "proj":
                        proj_of[layer, step[1]] = n_proj
                        n_proj += 1
                        projections.append(("mixer", (layer, step[1])))
                        if step[1] == "mem_v" or step[1][0] == "v":
                            dve_copies[layer, step[1]] = len(dve_copies) + 1
                        else:
                            act_copies[layer, step[1]] = len(act_copies) + 1
                    elif step[0] == "scores":
                        scores_count[layer, step[1]] = n_scores
                        n_scores += 1
                    elif step[0] == "turn":
                        new_job((layer, *step[1:]))
                        values_count[layer, step[1], step[2]] = n_values
                        n_values += 1
                        if kinds[layer] == "A" and step[1] >= 2:
                            rms_count[layer, step[1]] = n_rms
                            n_rms += 1
                    elif step[0] == "cat":
                        heads_jobs = [j for key, j in job_of.items() if len(key) == 3 and key[0] == layer
                                      and key[1] in head_groups(kinds[layer], step[1])]
                        cat_needs[layer, step[1]] = [max(j for j in heads_jobs if j % 2 == b)
                                                     for b in range(2) if any(j % 2 == b for j in heads_jobs)]
                        new_job(("cat", layer, step[1]))
                for t in range(TT):
                    for h in range(2):
                        new_job(("x", 3 * layer + 1, t, h))

    ctx = ExitStack()
    with ctx:
        def sb(name, shape, dt=F32):
            return ctx.enter_context(nc.sbuf_tensor(name, shape, dt))

        def sem(name):
            return ctx.enter_context(nc.semaphore(name))

        raw = [sb(f"raw{i}", [P, UNIT]) for i in range(RING)]
        w_hi = [sb(f"w_hi{i}", [P, UNIT], F32R) for i in range(RING)]
        w_lo = [sb(f"w_lo{i}", [P, UNIT], F32R) for i in range(RING)]
        x = sb("x", [P, TT, dm])
        x_t_hi = sb("x_t_hi", [P, KT, seq], F32R)
        x_t_lo = sb("x_t_lo", [P, KT, seq], F32R)
        mem_t_hi = sb("mem_t_hi", [P, KT, seq], F32R)
        mem_t_lo = sb("mem_t_lo", [P, KT, seq], F32R)
        act_hi = sb("act_hi", [P, KT, seq], F32R)
        act_lo = sb("act_lo", [P, KT, seq], F32R)
        wide = sb("wide", [P, TT, dm])
        gain = [sb(f"gain{i}", [P, 2, dm]) for i in range(2)]
        silu = sb("silu", [P, 2, seq])
        gated = sb("gated", [P, 2, seq])
        q_k = sb("q_k", [P, 2, 2, seq])
        k_win = sb("k_win", [P, 2, seq])
        k_mem = sb("k_mem", [P, 2, seq])
        q_mem = sb("q_mem", [P, 2, seq])
        v_tok = sb("v_tok", [P, TT, DIFF_HEADS * P])
        v_mem = sb("v_mem", [P, TT, 4 * HEAD])
        probs = sb("probs", [P, PROBS, 2, TT, seq])
        probs_t = sb("probs_t", [P, 2, TT, seq])
        ident = sb("ident", [P, P])
        minus_dist = sb("minus_dist", [P, TT, seq])
        minus_dist_win = sb("minus_dist_win", [P, TT, seq])
        squares = sb("squares", [P, 2, TT, P])
        bn = sb("bn", [P, 2, 6])
        mean_var = sb("mean_var", [P, TT, 2])
        var_eps = sb("var_eps", [P, TT])
        rstd = sb("rstd", [P, TT])
        minus_half = sb("minus_half", [P, TT])
        minus_max = sb("minus_max", [P, PROBS, 2, TT])
        sums = sb("sums", [P, PROBS, 2, TT])
        sink_exp = sb("sink_exp", [P, PROBS, 2, TT])
        inv = sb("inv", [P, PROBS, 2, TT])
        rms_sq = sb("rms_sq", [P, 2, TT])
        rms_eps = sb("rms_eps", [P, 2, TT])
        rms = sb("rms", [P, 2, TT])
        sink = sb("sink", [P, WIN_HEADS])
        minus_sink = sb("minus_sink", [P, WIN_HEADS])
        sub_gain = sb("sub_gain", [P, P])
        lam_in = sb("lam_in", [P, 4, HEAD])
        lam_prod = sb("lam_prod", [P, 2, HEAD])
        lam_dot = sb("lam_dot", [P, 2])
        lam_exp = sb("lam_exp", [P, 2])
        minus_lam = sb("minus_lam", [P, 1])

        Y = ctx.enter_context(nc.psum_tensor("Y", [P, TT, dm], F32))
        G = ctx.enter_context(nc.psum_tensor("G", [P, 2, 2, seq], F32))
        T = ctx.enter_context(nc.psum_tensor("T", [P, 2, 512], F32))

        raw_landed = [sem(f"raw_landed{i}") for i in range(RING)]
        hi_made = sem("hi_made")
        lo_made = sem("lo_made")
        unit_used = sem("unit_used")
        silu_made = sem("silu_made")
        gate_steps = sem("gate_steps")
        y_full = sem("y_full")
        turn_full = sem("turn_full")
        turn_copied = sem("turn_copied")
        turn_free = [sem(f"turn_free{i}") for i in range(2)]
        scores_full = sem("scores_full")
        scores_free = sem("scores_free")
        max_made = sem("max_made")
        exp_made = sem("exp_made")
        probs_made = sem("probs_made")
        values_full = sem("values_full")
        squares_made = sem("squares_made")
        rms_made = sem("rms_made")
        act_copied = sem("act_copied")
        dve_copied = sem("dve_copied")
        y_read = sem("y_read")
        var_made = sem("var_made")
        rstd_made = sem("rstd_made")
        x_made = sem("x_made")
        gain_landed = [sem(f"gain_landed{i}") for i in range(2)]
        x_landed = sem("x_landed")
        mem_landed = sem("mem_landed")
        small_landed = sem("small_landed")
        ident_made = sem("ident_made")
        dist_made = sem("dist_made")
        lam_dotted = sem("lam_dotted")
        lam_exped = sem("lam_exped")
        dve_done = sem("dve_done")
        pool_done = sem("pool_done")
        out_landed = sem("out_landed")

        block = ctx.enter_context(nc.Block())

        def at(value, per_turn, turn):
            return value if turn is None else value + turn * per_turn

        FFN_UNIT_STEP = 6

        def norm_after_ffn(layer, half):
            return 3 * layer + 2 * half

        @block.sync
        def _(sp):
            def load(u, turn=None):
                kind, layer, which, n = units[u]
                dst = raw[u % RING]
                done = raw_landed[u % RING]
                if u >= RING:
                    sp.wait_ge(lo_made, at(u - RING + 1, FFN_UNIT_STEP, turn))
                if kind == "w13":
                    src = w13_in[which][layer].rearrange("(k p) n -> p k n", p=P)
                    to = dst[:, :].rearrange("p (k g n) -> p g k n", k=KT, g=2)
                    for g in range(2):
                        col = at(g * ff + n * P, 4 * P, turn)
                        sp.dma_start(to[:, g], src[:, :, bass.ds(col, P)]).then_inc(done, 16)
                elif kind in ("w2", "out"):
                    w = w2_in[which][layer] if kind == "w2" else w_out[layer]
                    pair = n if kind == "w2" else which
                    src = w.rearrange("(m p) n -> p m n", p=P)
                    to = dst[:, :].rearrange("p (m n) -> p m n", m=2)
                    sp.dma_start(to, src[:, bass.ds(at(2 * pair, 4, turn), 2), :]).then_inc(done, 16)
                else:
                    name = which
                    if name in ("mem_k", "mem_v"):
                        w, cols = w_mem_kv[layer], [(4 * HEAD if name == "mem_v" else 0, 4 * HEAD)]
                    elif layer == 0:
                        w = a_w_in[0]
                        width = DIFF_HEADS * P
                        if name == "q_mem":
                            cols = [(3 * width, 256)]
                        elif name[0] == "v":
                            cols = [(2 * width + 256 * int(name[1]), 256)]
                        else:
                            cols = [(P * int(name[2]), P), (width + P * int(name[2]), P)]
                    else:
                        w = b_w_in[0]
                        width = WIN_HEADS * HEAD
                        if name == "q_mem":
                            cols = [(width + 512, 256)]
                        elif name == "k":
                            cols = [(width, 256)]
                        elif name == "v":
                            cols = [(width + 256, 256)]
                        else:
                            heads = [h for g in (2 * int(name[1]), 2 * int(name[1]) + 1) for h in window_heads(g)]
                            cols = [(h * HEAD, HEAD) for h in heads]
                    src = w.rearrange("(k p) n -> p k n", p=P)
                    to = dst[:, :].rearrange("p (k n) -> p k n", k=KT)
                    at_col = 0
                    for col, width in cols:
                        sp.dma_start(to[:, :, at_col:at_col + width], src[:, :, col:col + width]).then_inc(done, 16)
                        at_col += width

            for layer in range(depth):
                for half in range(2):
                    u0 = ffn_first_unit[layer, half]
                    for j in range(FFN_HEAD):
                        load(u0 + j)
                    with sp.Fori(0, FFN_TURNS) as turn:
                        for j in range(6):
                            load(u0 + FFN_HEAD + j, turn)
                    for j in range(FFN_HEAD + 6 * FFN_TURNS, 33):
                        load(u0 + j)
                    if half == 0:
                        for step in mixers[layer]:
                            if step[0] in ("proj", "out"):
                                load(mixer_unit[layer, step])
            norm = 3 * depth - 1
            for t in range(TT):
                for h in range(2):
                    sp.wait_ge(x_made, 4 * norm + 2 * t + h + 1)
                    sp.dma_start(out[0, t * P:(t + 1) * P, h * 512:(h + 1) * 512],
                                 x[:, t, h * 512:(h + 1) * 512]).then_inc(out_landed, 16)
            sp.wait_ge(out_landed, 16 * 2 * TT)

        @block.gpsimd
        def _(pool):
            count = [0]

            def link(ins):
                count[0] += 1
                ins.then_inc(pool_done, 1)
                pool.wait_ge(pool_done, count[0])

            link(pool.memset(ident[:, :], 0.0))
            pool.affine_select(out=ident[:, :], in_=ident[:, :], compare_op=ALU.not_equal, fill=1.0,
                               base=0, pattern=[[-1, P]], channel_multiplier=1).then_inc(ident_made, 1)
            pool.iota(minus_dist[:, :, :], [[P, TT], [-1, seq]], base=0, channel_multiplier=1,
                      allow_small_or_imprecise_dtypes=True).then_inc(dist_made, 1)
            link(pool.memset(minus_half[:, :], -0.5))

            def norm_rstd(norm):
                for t in range(TT):
                    pool.wait_ge(var_made, TT * norm + t + 1)
                    pool.tensor_tensor(rstd[:, t:t + 1], var_eps[:, t:t + 1], minus_half[:, 0:1],
                                       ALU.pow).then_inc(rstd_made, 1)

            for layer in range(depth):
                norm_rstd(3 * layer)
                for step in mixers[layer]:
                    if step[0] == "values" and (layer, step[1]) in rms_count:
                        n = rms_count[layer, step[1]]
                        pool.wait_ge(squares_made, 2 * n + 2)
                        link(pool.tensor_scalar(rms_eps[:, n % 2], rms_sq[:, n % 2], 1.0 / P, LN_EPS,
                                                ALU.mult, ALU.add))
                        pool.tensor_tensor(rms[:, n % 2], rms_eps[:, n % 2], minus_half[:, :],
                                           ALU.pow).then_inc(rms_made, 1)
                norm_rstd(3 * layer + 1)
                norm_rstd(3 * layer + 2)

        @block.scalar
        def _(act):
            def load_gain(norm):
                i, layer = norm % 3, norm // 3
                buf = norm % 2
                for j, src in enumerate((ln_g[i], ln_b[i])):
                    act.dma_start(gain[buf][:, j, :], src[layer:layer + 1, :].to_broadcast([P, dm]))\
                       .then_inc(gain_landed[buf], 16)

            def split_hi(u, turn=None):
                if u >= n_units:
                    return
                per = 16 * 2 * dmas_of(units[u])
                act.wait_ge(raw_landed[u % RING], at(landed_at[u], per, turn))
                if u >= RING:
                    act.wait_ge(unit_used, at(u - RING + 1, FFN_UNIT_STEP, turn))
                act.activation(w_hi[u % RING][:, :], raw[u % RING][:, :], ACT.Copy).then_inc(hi_made, 1)

            def copy_turned(job, dst, shape=None):
                act.wait_ge(turn_full, job + 1)
                src = T[:, job % 2, :]
                if shape:
                    src = src.rearrange("p (a b) -> p a b", a=shape)
                act.activation(dst, src, ACT.Copy).then_inc(turn_copied, 1)

            def ffn(layer, half):
                u0, p0 = ffn_first_unit[layer, half], ffn_first_proj[layer, half]
                plan = plan_ffn()

                def after(j, turn=None):
                    kind, n = plan[j]
                    if kind == "w13":
                        p = p0 + n
                        act.wait_ge(unit_used, at(u0 + j + 1, FFN_UNIT_STEP, turn))
                        act.activation(silu[:, p % 2, :], G[:, p % 2, 0, :], ACT.Silu).then_inc(silu_made, 1)
                    split_hi(u0 + j + RING, turn)

                for j in range(FFN_HEAD):
                    after(j)
                if (layer, half) == (0, 0):
                    for t in range(TT):
                        for h in range(2):
                            copy_turned(job_of["mem", t, h], mem_t_hi[:, 4 * h:4 * h + 4, t * P:(t + 1) * P], 4)
                with act.Fori(0, FFN_TURNS) as turn:
                    for j in range(FFN_HEAD, FFN_HEAD + 6):
                        after(j, turn)
                for j in range(FFN_HEAD + 6 * FFN_TURNS, 31):
                    after(j)

            def norm(n):
                if n < 3 * depth - 1:
                    if n % 3 == 0:
                        split_hi(last_unit[n] + RING - 1)
                        split_hi(last_unit[n] + RING)
                    for t in range(TT):
                        if n % 3:
                            split_hi(last_unit[n] + RING - 1 + t)
                        for h in range(2):
                            copy_turned(job_of["x", n, t, h],
                                        x_t_hi[:, 4 * h:4 * h + 4, t * P:(t + 1) * P], 4)
                    if n + 2 < 3 * depth:
                        load_gain_after = x_made
                        act.wait_ge(load_gain_after, 4 * (n + 1))
                        load_gain(n + 2)

            def mixer(layer):
                if kinds[layer] == "A":
                    act.wait_ge(lam_dotted, 1)
                    act.activation(lam_exp[:, :], lam_dot[:, :], ACT.Exp).then_inc(lam_exped, 1)
                for step in mixers[layer]:
                    if step[0] == "proj":
                        name = step[1]
                        u, p = mixer_unit[layer, step], proj_of[layer, name]
                        if (layer, name) in act_copies:
                            act.wait_ge(unit_used, u + 1)
                            bank = G[:, p % 2, :, :]
                            scale = HEAD ** -0.5
                            if name == "mem_k":
                                last = act.activation(k_mem[:, :, :], bank, ACT.Copy)
                            elif name == "q_mem":
                                last = act.activation(q_mem[:, :, :], bank, ACT.Copy, scale=scale)
                            elif name == "k":
                                last = act.activation(k_win[:, :, :], bank, ACT.Copy)
                            elif kinds[layer] == "B":
                                j = int(name[1])
                                if j >= 2:
                                    act.wait_ge(scores_full, scores_count[layer, 2 + 2 * (j - 2) + 1] + 1)
                                last = act.activation(q_k[:, j % 2, :, :], bank, ACT.Copy, scale=scale)
                            else:
                                h = int(name[2])
                                if h >= 2:
                                    act.wait_ge(scores_full, scores_count[layer, 2 + h - 2] + 1)
                                act.activation(q_k[:, h % 2, 0, :], bank[:, 0, :], ACT.Copy, scale=scale)
                                last = act.activation(q_k[:, h % 2, 1, :], bank[:, 1, :], ACT.Copy)
                            last.then_inc(act_copied, 1)
                        split_hi(u + RING)
                    elif step[0] == "scores":
                        g = step[1]
                        n = scores_count[layer, g]
                        b = n % PROBS
                        act.wait_ge(max_made, n + 1)
                        for c in range(2):
                            for t in range(TT):
                                last = act.activation(probs[:, b, c, t, :], probs[:, b, c, t, :], ACT.Exp,
                                                      bias=minus_max[:, b, c, t:t + 1],
                                                      accum_out=sums[:, b, c, t:t + 1])
                            if kinds[layer] == "B" and g >= 2:
                                h = window_heads(g - 2)[c]
                                last = act.activation(sink_exp[:, b, c, :], minus_max[:, b, c, :], ACT.Exp,
                                                      bias=sink[:, h:h + 1])
                        last.then_inc(exp_made, 1)
                    elif step[0] == "turn":
                        job = job_of[layer, step[1], step[2]]
                        n = values_count[layer, step[1], step[2]]
                        copy_turned(job, probs_t[:, n % 2].rearrange("p a b -> p (a b)"))
                    elif step[0] == "values":
                        if (layer, step[1]) in rms_count:
                            n = rms_count[layer, step[1]]
                            job = job_of[layer, step[1], step[2]]
                            act.wait_ge(values_full, values_count[layer, step[1], step[2]] + 1)
                            if n >= 2:
                                act.wait_ge(rms_made, n - 1)
                            for t in range(TT):
                                act.activation(squares[:, n % 2, t, :], T[:, job % 2, t * P:(t + 1) * P], ACT.Square,
                                               accum_out=rms_sq[:, n % 2, t:t + 1]).then_inc(squares_made, 1)
                    elif step[0] == "cat":
                        kp = step[1]
                        copy_turned(job_of["cat", layer, kp],
                                    act_hi[:, 2 * kp:2 * kp + 2, :].rearrange("p a b -> p (a b)"))
                    elif step[0] == "out" and step[1] in (3, 0):
                        split_hi(mixer_unit[layer, step] + RING)

            for t in range(TT):
                act.dma_start(x[:, t, :], x_in[0, t * P:(t + 1) * P, :]).then_inc(x_landed, 16)
            for t in range(TT):
                for h in range(2):
                    copy_turned(job_of["x", -1, t, h], x_t_hi[:, 4 * h:4 * h + 4, t * P:(t + 1) * P], 4)
            for u in range(RING):
                split_hi(u)
            for t in range(TT):
                act.dma_start(wide[:, t, :], mem_in[0, t * P:(t + 1) * P, :]).then_inc(mem_landed, 16)
            for i, v in enumerate(lambdas):
                act.dma_start(lam_in[:, i, :], v[0:1, :].to_broadcast([P, HEAD])).then_inc(small_landed, 16)
            act.dma_start(sub_gain[:, :], subln_g[0:1, :].to_broadcast([P, P])).then_inc(small_landed, 16)
            act.dma_start(sink[:, :], b_sink[0:1, :].to_broadcast([P, WIN_HEADS])).then_inc(small_landed, 16)
            load_gain(0)
            load_gain(1)
            for layer in range(depth):
                ffn(layer, 0)
                norm(3 * layer)
                mixer(layer)
                norm(3 * layer + 1)
                ffn(layer, 1)
                norm(3 * layer + 2)

        @block.vector
        def _(dve):
            count = [0]

            def link(ins):
                count[0] += 1
                ins.then_inc(dve_done, 1)
                dve.wait_ge(dve_done, count[0])

            def split_lo(u, turn=None):
                if u >= n_units:
                    return
                dve.wait_ge(hi_made, at(u + 1, FFN_UNIT_STEP, turn))
                dve.tensor_tensor(w_lo[u % RING][:, :], raw[u % RING][:, :],
                                  w_hi[u % RING][:, :].bitcast(F32), ALU.subtract).then_inc(lo_made, 1)

            def turned_lo(job, hi, lo, shape=None):
                dve.wait_ge(turn_copied, job + 1)
                src = T[:, job % 2, :]
                if shape:
                    src = src.rearrange("p (a b) -> p a b", a=shape)
                dve.tensor_tensor(lo, src, hi.bitcast(F32), ALU.subtract).then_inc(turn_free[job % 2], 1)

            def x_turned_lo(key, hi, lo):
                _, t, h = key[-3:]
                part = (slice(None), slice(4 * h, 4 * h + 4), slice(t * P, (t + 1) * P))
                turned_lo(job_of[key], hi[part], lo[part], 4)

            def ffn(layer, half):
                u0, p0 = ffn_first_unit[layer, half], ffn_first_proj[layer, half]
                chunk0 = FF_CHUNKS * (2 * layer + half)
                plan = plan_ffn()

                def after(j, turn=None):
                    kind, n = plan[j]
                    if kind == "w13":
                        b, slot, c = (p0 + n) % 2, n % 4, chunk0 + n
                        dve.wait_ge(silu_made, at(c + 1, 4, turn))
                        dve.tensor_tensor(gated[:, b, :], silu[:, b, :], G[:, b, 1, :], ALU.mult)\
                           .then_inc(gate_steps, 1)
                        dve.wait_ge(gate_steps, at(3 * c + 1, 12, turn))
                        dve.tensor_copy(act_hi[:, slot, :], gated[:, b, :]).then_inc(gate_steps, 1)
                        dve.wait_ge(gate_steps, at(3 * c + 2, 12, turn))
                        dve.tensor_tensor(act_lo[:, slot, :], gated[:, b, :], act_hi[:, slot, :].bitcast(F32),
                                          ALU.subtract).then_inc(gate_steps, 1)
                    split_lo(u0 + j + RING, turn)

                for j in range(FFN_HEAD):
                    after(j)
                if (layer, half) == (0, 0):
                    for t in range(TT):
                        for h in range(2):
                            x_turned_lo(("mem", t, h), mem_t_hi, mem_t_lo)
                with dve.Fori(0, FFN_TURNS) as turn:
                    for j in range(FFN_HEAD, FFN_HEAD + 6):
                        after(j, turn)
                for j in range(FFN_HEAD + 6 * FFN_TURNS, 31):
                    after(j)

            def norm(n):
                c = (1.0 if n % 3 == 1 else 0.5) / alpha
                g = gain[n % 2]
                dve.wait_ge(gain_landed[n % 2], 32 * (n // 2 + 1))
                for t in range(TT):
                    if t == 0:
                        dve.wait_ge(y_full, n + 1)
                    else:
                        dve.wait_ge(unit_used, last_unit[n] + 1)
                    dve.scalar_tensor_tensor(out=wide[:, t, :], in0=Y[:, t, :], scalar=c, in1=x[:, t, :],
                                             op0=ALU.mult, op1=ALU.add).then_inc(y_read, 1)
                    dve.wait_ge(y_read, TT * n + t + 1)
                    for h in range(2):
                        last = dve.bn_stats(bn[:, h, :], wide[:, t, h * 512:(h + 1) * 512])
                    link(last)
                    link(dve.bn_aggr(mean_var[:, t, :], bn[:, :, :].rearrange("p a b -> p (a b)")))
                    dve.tensor_scalar(var_eps[:, t:t + 1], mean_var[:, t, 1:2], LN_EPS / alpha ** 2, None,
                                      ALU.add).then_inc(var_made, 1)
                    link(dve.scalar_tensor_tensor(out=wide[:, t, :], in0=wide[:, t, :], scalar=mean_var[:, t, 0:1],
                                                  in1=g[:, 0, :], op0=ALU.subtract, op1=ALU.mult))
                    dve.wait_ge(rstd_made, TT * n + t + 1)
                    for h in range(2):
                        part = slice(h * 512, (h + 1) * 512)
                        dve.scalar_tensor_tensor(out=x[:, t, part], in0=wide[:, t, part], scalar=rstd[:, t:t + 1],
                                                 in1=g[:, 1, part], op0=ALU.mult, op1=ALU.add).then_inc(x_made, 1)
                    if n % 3 == 0:
                        split_lo(last_unit[n] + RING - 1 + t)
                if n < 3 * depth - 1:
                    for t in range(TT):
                        for h in range(2):
                            x_turned_lo(("x", n, t, h), x_t_hi, x_t_lo)
                if n % 3:
                    split_lo(last_unit[n] + RING - 1)
                    split_lo(last_unit[n] + RING)

            def mixer(layer):
                a = kinds[layer] == "A"
                if a:
                    dve.wait_ge(small_landed, 16 * 6)
                    for i in range(2):
                        last = dve.tensor_tensor(lam_prod[:, i, :], lam_in[:, 2 * i, :], lam_in[:, 2 * i + 1, :], ALU.mult)
                    link(last)
                    dve.tensor_reduce(lam_dot[:, :], lam_prod[:, :, :], AX_X, ALU.add).then_inc(lam_dotted, 1)
                    dve.tensor_scalar(minus_sink[:, :], sink[:, :], -1.0, None, ALU.mult)
                    link(dve.tensor_scalar(sub_gain[:, :], sub_gain[:, :], 1.0 - LAM_INIT, None, ALU.mult))
                    dve.wait_ge(lam_exped, 1)
                    link(dve.tensor_tensor(minus_lam[:, :], lam_exp[:, 1:2], lam_exp[:, 0:1], ALU.subtract))
                    link(dve.tensor_scalar(minus_lam[:, :], minus_lam[:, :], -LAM_INIT, None, ALU.add))
                for step in mixers[layer]:
                    if step[0] == "proj":
                        name = step[1]
                        u, p = mixer_unit[layer, step], proj_of[layer, name]
                        if (layer, name) in dve_copies:
                            dve.wait_ge(unit_used, u + 1)
                            if name == "mem_v":
                                dst = v_mem[:, :, :]
                            elif a:
                                dst = v_tok[:, :, 256 * int(name[1]):256 * int(name[1]) + 256]
                            else:
                                dst = v_tok[:, :, 0:256]
                            dve.tensor_copy(dst, G[:, p % 2, :, :]).then_inc(dve_copied, 1)
                        split_lo(u + RING)
                    elif step[0] == "scores":
                        g = step[1]
                        n = scores_count[layer, g]
                        b = n % PROBS
                        dve.wait_ge(scores_full, n + 1)
                        if n >= PROBS:
                            g_before = [s for s, m in scores_count.items() if m == n - PROBS][0]
                            dve.wait_ge(turn_full, last_job_of(*g_before) + 1)
                        for c in range(2):
                            src = Y[:, n % 2, c * 512:(c + 1) * 512]
                            dst = probs[:, b, c].rearrange("p a b -> p (a b)")
                            if g < 2:
                                last = dve.tensor_copy(dst, src)
                            else:
                                s = slope(DIFF_HEADS, g - 2) if a else slope(WIN_HEADS, window_heads(g - 2)[c])
                                dist = (minus_dist if a else minus_dist_win)[:, :, :]
                                last = dve.scalar_tensor_tensor(
                                    out=dst, in0=dist.rearrange("p a b -> p (a b)"), scalar=s, in1=src,
                                    op0=ALU.mult, op1=ALU.add)
                        last.then_inc(scores_free, 1)
                        dve.wait_ge(scores_free, n + 1)
                        flat = minus_max[:, b].rearrange("p c t -> p (c t)")
                        top = dve.tensor_reduce(flat, probs[:, b].rearrange("p c t k -> p (c t) k"), AX_X,
                                                ALU.max, negate=True)
                        if not a and g >= 2:
                            link(top)
                            for c in range(2):
                                h = window_heads(g - 2)[c]
                                top = dve.tensor_scalar(minus_max[:, b, c, :], minus_max[:, b, c, :],
                                                        minus_sink[:, h:h + 1], None, ALU.min)
                        top.then_inc(max_made, 1)
                    elif step[0] == "probs":
                        g = step[1]
                        n = scores_count[layer, g]
                        b = n % PROBS
                        dve.wait_ge(exp_made, n + 1)
                        flat = lambda s: s[:, b].rearrange("p c t -> p (c t)")
                        if not a and g >= 2:
                            link(dve.tensor_tensor(flat(sums), flat(sums), flat(sink_exp), ALU.add))
                        if not a or g < 2:
                            dve.reciprocal(flat(inv), flat(sums)).then_inc(probs_made, 1)
                            continue
                        link(dve.reciprocal(flat(inv), flat(sums)))
                        link(dve.tensor_scalar(inv[:, b, 1, :], inv[:, b, 1, :], minus_lam[:, 0:1], None, ALU.mult))
                        for t in range(TT):
                            last = dve.tensor_scalar(probs[:, b, 1, t, :], probs[:, b, 1, t, :],
                                                     inv[:, b, 1, t:t + 1], None, ALU.mult)
                        link(last)
                        for t in range(TT):
                            last = dve.scalar_tensor_tensor(
                                out=probs[:, b, 0, t, :], in0=probs[:, b, 0, t, :], scalar=inv[:, b, 0, t:t + 1],
                                in1=probs[:, b, 1, t, :], op0=ALU.mult, op1=ALU.add)
                        last.then_inc(probs_made, 1)
                    elif step[0] == "values":
                        g, c = step[1:]
                        job, n = job_of[layer, g, c], values_count[layer, g, c]
                        b = scores_count[layer, g] % PROBS
                        bank = T[:, job % 2, :]
                        if (layer, g) in rms_count:
                            r = rms_count[layer, g]
                            dve.wait_ge(rms_made, r + 1)
                            col = (g - 2) * P
                            for t in range(TT):
                                last = dve.scalar_tensor_tensor(
                                    out=wide[:, t, col:col + P], in0=bank[:, t * P:(t + 1) * P],
                                    scalar=rms[:, r % 2, t:t + 1], in1=sub_gain[:, :], op0=ALU.mult, op1=ALU.mult)
                        else:
                            dve.wait_ge(values_full, n + 1)
                            head = WIN_HEADS + 2 * g + c if g < 2 else window_heads(g - 2)[c]
                            for t in range(TT):
                                last = dve.tensor_scalar(
                                    wide[:, t, head * HEAD:(head + 1) * HEAD], bank[:, t * HEAD:(t + 1) * HEAD],
                                    inv[:, b, c, t:t + 1], None, ALU.mult)
                        last.then_inc(turn_free[job % 2], 1)
                    elif step[0] == "cat":
                        kp = step[1]
                        part = (slice(None), slice(2 * kp, 2 * kp + 2), slice(None))
                        turned_lo(job_of["cat", layer, kp], act_hi[part].rearrange("p a b -> p (a b)"),
                                  act_lo[part].rearrange("p a b -> p (a b)"))
                    elif step[0] == "out" and step[1] in (3, 0):
                        split_lo(mixer_unit[layer, step] + RING)

            def last_job_of(layer, g):
                return max(j for key, j in job_of.items() if key[:2] == (layer, g) and len(key) == 3)

            dve.wait_ge(dist_made, 1)
            flat = lambda s: s[:, :, :].rearrange("p a b -> p (a b)")
            link(dve.scalar_tensor_tensor(out=flat(minus_dist), in0=flat(minus_dist), scalar=-1.0,
                                          in1=flat(minus_dist), op0=ALU.mult, op1=ALU.min))
            link(dve.tensor_scalar(flat(minus_dist_win), flat(minus_dist), -float(WINDOW), NEG,
                                   ALU.is_lt, ALU.mult))
            link(dve.tensor_tensor(flat(minus_dist_win), flat(minus_dist_win), flat(minus_dist), ALU.add))
            for t in range(TT):
                for h in range(2):
                    x_turned_lo(("x", -1, t, h), x_t_hi, x_t_lo)
            for u in range(RING):
                split_lo(u)
            for layer in range(depth):
                ffn(layer, 0)
                norm(3 * layer)
                mixer(layer)
                norm(3 * layer + 1)
                ffn(layer, 1)
                norm(3 * layer + 2)

        @block.tensor
        def _(pe):
            PASSES = [(0, 0), (0, 1), (1, 0)]

            def job_done(job):
                pe.wait_ge(turn_free[job % 2], job // 2 + 1)

            def start_job(job):
                if job >= 2:
                    job_done(job - 2)

            def turn_x(key, src):
                _, t, h = key[-3:]
                job = job_of[key]
                start_job(job)
                for k in range(4):
                    col = (4 * h + k) * P
                    last = pe.transpose(T[:, job % 2, k * P:(k + 1) * P], src[:, t, col:col + P], ident[:, :])
                last.then_inc(turn_full, 1)

            def wait_weights(u, turn=None):
                pe.wait_ge(lo_made, at(u + 1, FFN_UNIT_STEP, turn))

            def feature_major(u, p, src_hi, src_lo, gated):
                moving = (src_hi, src_lo)
                view = [w[u % RING][:, :].rearrange("p (k g n) -> p k g n", k=KT, g=2) for w in (w_hi, w_lo)]
                for g in range(2):
                    for k in range(KT):
                        for i, (wi, xi) in enumerate(PASSES):
                            last = pe.matmul(G[:, p % 2, g, :], view[wi][:, k, g, :], moving[xi][:, k, :],
                                             start=(k == 0 and i == 0), stop=(k == KT - 1 and i == 2))
                last.then_inc(unit_used, 1)

            def token_major(u, p, src_hi, src_lo):
                stationary = (src_hi, src_lo)
                view = [w[u % RING][:, :].rearrange("p (k n) -> p k n", k=KT) for w in (w_hi, w_lo)]
                for t in range(TT):
                    for k in range(KT):
                        for i, (wi, xi) in enumerate(PASSES):
                            last = pe.matmul(G[:, p % 2, t, :], stationary[xi][:, k, t * P:(t + 1) * P],
                                             view[wi][:, k, :], start=(k == 0 and i == 0),
                                             stop=(k == KT - 1 and i == 2))
                last.then_inc(unit_used, 1)

            def accumulate(u, slots, t, first, stop):
                view = [w[u % RING][:, :].rearrange("p (m n) -> p m n", m=2) for w in (w_hi, w_lo)]
                stationary = (act_hi, act_lo)
                for m in range(2):
                    for half in range(2):
                        cols = slice(half * 512, (half + 1) * 512)
                        for i, (wi, xi) in enumerate(PASSES):
                            last = pe.matmul(Y[:, t, cols], stationary[xi][:, slots[m], t * P:(t + 1) * P],
                                             view[wi][:, m, cols], start=(first and m == 0 and i == 0),
                                             stop=(stop and m == 1 and i == 2))
                return last

            def bank_free(p, turn=None):
                if p < 2:
                    return
                stage, which = projections[p - 2]
                if stage == "chunk":
                    pe.wait_ge(gate_steps, at(3 * which + 1, 12, turn))
                elif which in act_copies:
                    pe.wait_ge(act_copied, act_copies[which])
                else:
                    pe.wait_ge(dve_copied, dve_copies[which])

            def ffn(layer, half, y_done):
                u0, p0 = ffn_first_unit[layer, half], ffn_first_proj[layer, half]
                chunk0 = FF_CHUNKS * (2 * layer + half)
                plan = plan_ffn()

                def unit(j, turn=None):
                    kind, n = plan[j]
                    u = u0 + j
                    wait_weights(u, turn)
                    if kind == "w13":
                        bank_free(p0 + n, turn)
                        feature_major(u, p0 + n, x_t_hi, x_t_lo, True)
                    else:
                        pe.wait_ge(gate_steps, at(3 * (chunk0 + 2 * n + 2), 12, turn))
                        slots = [(2 * n) % 4, (2 * n + 1) % 4]
                        if n == 0 and y_done:
                            pe.wait_ge(y_read, y_done)
                        for t in range(TT):
                            last = accumulate(u, slots, t, first=(turn is None and n == 0), stop=False)
                        last.then_inc(unit_used, 1)

                for j in range(FFN_HEAD):
                    unit(j)
                if (layer, half) == (0, 0):
                    pe.wait_ge(mem_landed, 16 * TT)
                    for t in range(TT):
                        for h in range(2):
                            turn_x(("mem", t, h), wide)
                with pe.Fori(0, FFN_TURNS) as turn:
                    for j in range(FFN_HEAD, FFN_HEAD + 6):
                        unit(j, turn)
                j = FFN_HEAD + 6 * FFN_TURNS
                unit(j)
                unit(j + 1)
                wait_weights(u0 + j + 2)
                pe.wait_ge(gate_steps, 3 * (chunk0 + FF_CHUNKS - 2))
                for t in range(TT):
                    last = accumulate(u0 + j + 2, [(FF_CHUNKS - 4) % 4, (FF_CHUNKS - 3) % 4], t, False, False)
                    if t == TT - 1:
                        last.then_inc(unit_used, 1)
                    if t == 0:
                        wait_weights(u0 + j + 3)
                        pe.wait_ge(gate_steps, 3 * (chunk0 + FF_CHUNKS))
                    last = accumulate(u0 + j + 3, [(FF_CHUNKS - 2) % 4, (FF_CHUNKS - 1) % 4], t, False, True)
                    last.then_inc(y_full if t == 0 else unit_used, 1)

            def turn_norm(n):
                for t in range(TT):
                    for h in range(2):
                        pe.wait_ge(x_made, 4 * n + 2 * t + h + 1)
                        turn_x(("x", n, t, h), x)

            def x_turned(n):
                job_done(job_of["x", n, 1, 0])
                job_done(job_of["x", n, 1, 1])

            def mixer(layer):
                a = kinds[layer] == "A"
                norm = 3 * layer
                turned = False
                outs = [s for s in mixers[layer] if s[0] == "out"]
                for step in mixers[layer]:
                    if step[0] == "proj":
                        name = step[1]
                        u, p = mixer_unit[layer, step], proj_of[layer, name]
                        if name == "q_mem":
                            turn_norm(norm)
                            x_turned(norm)
                        wait_weights(u)
                        bank_free(p)
                        if name == "mem_k":
                            feature_major(u, p, mem_t_hi, mem_t_lo, False)
                        elif name == "mem_v":
                            token_major(u, p, mem_t_hi, mem_t_lo)
                        elif name[0] == "v":
                            token_major(u, p, x_t_hi, x_t_lo)
                        else:
                            feature_major(u, p, x_t_hi, x_t_lo, False)
                    elif step[0] == "scores":
                        g = step[1]
                        n = scores_count[layer, g]
                        b = n % 2
                        if g < 2:
                            pe.wait_ge(y_read, TT * (norm + 1))
                            pe.wait_ge(act_copied, act_copies[layer, "q_mem"])
                            q, k = q_mem[:, g, :], k_mem[:, g, :]
                        elif a:
                            pe.wait_ge(act_copied, act_copies[layer, f"qk{g - 2}"])
                            q, k = q_k[:, g % 2, 0, :], q_k[:, g % 2, 1, :]
                        else:
                            j = (g - 2) // 2
                            pe.wait_ge(act_copied, act_copies[layer, f"q{j}"])
                            q, k = q_k[:, j % 2, g % 2, :], k_win[:, (g - 2) // 3, :]
                        if n >= 2:
                            pe.wait_ge(scores_free, n - 1)
                        for c in range(2):
                            rows = slice(c * HEAD, (c + 1) * HEAD)
                            for t in range(TT):
                                last = pe.matmul(Y[:, b, c * 512 + t * seq:c * 512 + (t + 1) * seq],
                                                 q[rows, t * P:(t + 1) * P], k[rows, :], start=True, stop=True)
                        last.then_inc(scores_full, 1)
                    elif step[0] == "turn":
                        g, c = step[1:]
                        job = job_of[layer, g, c]
                        n = scores_count[layer, g]
                        pe.wait_ge(probs_made, n + 1)
                        start_job(job)
                        for kt in range(TT):
                            for t in range(TT):
                                at_col = kt * seq + t * P
                                last = pe.transpose(T[:, job % 2, at_col:at_col + P],
                                                    probs[:, n % PROBS, c, t, kt * P:(kt + 1) * P], ident[:, :])
                        last.then_inc(turn_full, 1)
                    elif step[0] == "values":
                        g, c = step[1:]
                        job, n = job_of[layer, g, c], values_count[layer, g, c]
                        pe.wait_ge(turn_copied, job + 1)
                        if g < 2:
                            pe.wait_ge(dve_copied, dve_copies[layer, "mem_v"])
                            v, width = v_mem[:, :, (2 * g + c) * HEAD:(2 * g + c + 1) * HEAD], HEAD
                        elif a:
                            h = g - 2
                            pe.wait_ge(dve_copied, dve_copies[layer, f"v{h // 2}"])
                            v, width = v_tok[:, :, h * P:(h + 1) * P], P
                        else:
                            kv = window_heads(g - 2)[c] // WIN_GROUP
                            pe.wait_ge(dve_copied, dve_copies[layer, "v"])
                            v, width = v_tok[:, :, kv * HEAD:(kv + 1) * HEAD], HEAD
                        for t in range(TT):
                            for kt in range(TT):
                                last = pe.matmul(T[:, job % 2, t * width:(t + 1) * width],
                                                 probs_t[:, n % 2, kt, t * P:(t + 1) * P], v[:, kt, :],
                                                 start=(kt == 0), stop=(kt == TT - 1))
                        last.then_inc(values_full, 1)
                    elif step[0] == "cat":
                        kp = step[1]
                        job = job_of["cat", layer, kp]
                        for job_before in cat_needs[layer, kp]:
                            job_done(job_before)
                        start_job(job)
                        for m in range(2):
                            for t in range(TT):
                                col = (2 * kp + m) * P
                                last = pe.transpose(T[:, job % 2, m * seq + t * P:m * seq + (t + 1) * P],
                                                    wide[:, t, col:col + P], ident[:, :])
                        last.then_inc(turn_full, 1)
                    elif step[0] == "out":
                        kp = step[1]
                        u = mixer_unit[layer, step]
                        wait_weights(u)
                        job_done(job_of["cat", layer, kp])
                        if step == outs[0]:
                            pe.wait_ge(scores_free, max(m for (l, _), m in scores_count.items() if l == layer) + 1)
                        if step in outs[:2]:
                            for t in range(TT):
                                last = accumulate(u, [2 * kp, 2 * kp + 1], t, first=(step == outs[0]), stop=False)
                            last.then_inc(unit_used, 1)
                        elif step == outs[3]:
                            u3 = mixer_unit[layer, outs[2]]
                            kp3 = outs[2][1]
                            wait_weights(u3)
                            job_done(job_of["cat", layer, kp3])
                            for t in range(TT):
                                last = accumulate(u3, [2 * kp3, 2 * kp3 + 1], t, False, False)
                                if t == TT - 1:
                                    last.then_inc(unit_used, 1)
                                last = accumulate(u, [2 * kp, 2 * kp + 1], t, False, True)
                                last.then_inc(y_full if t == 0 else unit_used, 1)

            pe.wait_ge(ident_made, 1)
            pe.wait_ge(x_landed, 16 * TT)
            for t in range(TT):
                for h in range(2):
                    turn_x(("x", -1, t, h), x)
            x_turned(-1)
            for layer in range(depth):
                ffn(layer, 0, TT * 3 * layer)
                mixer(layer)
                turn_norm(3 * layer + 1)
                x_turned(3 * layer + 1)
                ffn(layer, 1, TT * (3 * layer + 2))
                if layer < depth - 1:
                    turn_norm(3 * layer + 2)
                    x_turned(3 * layer + 2)


def window_heads(g):
    first = g % 3 + 6 * (g // 3)
    return first, first + WIN_GROUP


_INS = ["x", "mem", "ffn1_w13", "ffn1_w2", "ln1_g", "ln1_b", "w_mem_kv", "w_out", "ln2_g", "ln2_b",
        "ffn2_w13", "ffn2_w2", "ln3_g", "ln3_b", "a_w_in", "a_lambda_q1", "a_lambda_k1", "a_lambda_q2",
        "a_lambda_k2", "a_subln_g", "b_w_in", "b_sink"]


def kernel(**inputs):
    import numpy as _np
    import concourse.bacc as _bacc
    from concourse.bass_utils import run_bass_kernel_spmd as _run

    nc = _bacc.Bacc("TRN2", target_bir_lowering=False, num_devices=1)
    arrays, a = {}, {}
    for name in _INS:
        v = _np.ascontiguousarray(inputs[name])
        arrays[f"in_{name}"] = v
        a[name] = nc.dram_tensor(f"in_{name}", v.shape, mybir.dt.from_np(v.dtype), kind="ExternalInput").ap()
    out = nc.dram_tensor("out", arrays["in_x"].shape, F32, kind="ExternalOutput").ap()
    build(nc, a["x"], a["mem"], [a["ffn1_w13"], a["ffn2_w13"]], [a["ffn1_w2"], a["ffn2_w2"]],
          [a["ln1_g"], a["ln2_g"], a["ln3_g"]], [a["ln1_b"], a["ln2_b"], a["ln3_b"]], a["w_mem_kv"],
          a["w_out"], a["a_w_in"], [a["a_lambda_q1"], a["a_lambda_k1"], a["a_lambda_q2"], a["a_lambda_k2"]],
          a["a_subln_g"], a["b_w_in"], a["b_sink"], out)
    r = _run(nc, [arrays], core_ids=[0])
    return r.results[0]["out"]
```

```python
import math
from contextlib import ExitStack

import concourse.bass as bass
from concourse import mybir

F32 = mybir.dt.float32
F32R = mybir.dt.float32r
ALU = mybir.AluOpType
ACT = mybir.ActivationFunctionType
AX_X = mybir.AxisListType.X

P = 128
RING = 3
UNIT = 2048
HEAD = 64
NEG = -1e30
LN_EPS = 1e-5

DIFF_HEADS = 6
WIN_HEADS = 12
WIN_GROUP = 3
WINDOW = 128
OUT_ORDER = [3, 0, 1, 2]
PROBS = 4
LAM_INIT = 0.8 - 0.6 * math.exp(-0.3 * 0)


def slope(n_heads, head):
    return float(2.0 ** (-8.0 * (head + 1) / n_heads))



def head_groups(kind, pair):
    if pair == 3:
        return {0, 1}
    if kind == "A":
        return {2 + 2 * pair, 3 + 2 * pair}
    heads = range(4 * pair, 4 * pair + 4)
    return {2 + g for g in range(6) if set(window_heads(g)) & set(heads)}


def unit_names(step):
    if step[0] == "outs":
        return step[1:]
    return step[1:2] if step[0] in ("proj", "out") and step[2] == 0 else ()


def plan_mixer(kind):
    if kind == "A":
        order = ["mem_k", "mem_v", "q_mem", "qk0", "qk1", "v0", "qk2", "qk3", "v1", "qk4", "qk5", "v2"]
        gives = {"q_mem": [0, 1]} | {f"qk{h}": [2 + h] for h in range(6)}
        values_of = lambda g: "mem_v" if g < 2 else f"v{(g - 2) // 2}"
        scores_to_turn = 2
    else:
        order = ["mem_k", "mem_v", "q_mem", "k", "q0", "q1", "v", "q2"]
        gives = {"q_mem": [0, 1]} | {f"q{j}": [2 + 2 * j, 3 + 2 * j] for j in range(3)}
        values_of = lambda g: "mem_v" if g < 2 else "v"
        scores_to_turn = 1
    halves = lambda g: [0] if kind == "A" and g >= 2 else [0, 1]
    pieces = [("proj", name, half) for name in order for half in range(2)]
    pieces += [("out", n, t) for n in OUT_ORDER[:2] for t in range(2)]
    last_proj = 2 * len(order) - 1

    steps = []
    to_score, to_turn, to_multiply, to_cat = [], [], [], list(OUT_ORDER)
    finished, done, to_lo = {}, {}, []
    for i, piece in enumerate(pieces + [("end",)]):
        last = piece[0] == "end"
        if not last:
            steps.append(piece)
        if i >= last_proj:
            ready = [n for n in to_cat if all(done.get(g, i) < i for g in head_groups(kind, n))][:2]
            steps += [("cat", n) for n in ready]
            to_cat = [n for n in to_cat if n not in ready]
        while to_multiply and finished.get(values_of(to_multiply[0][0]), i) < i and to_multiply[0][2] < i:
            g, c, _ = to_multiply.pop(0)
            steps.append(("values", g, c))
            done[g] = i
        scored = []
        while to_score and (to_score[0][1] < i and not scored or i == last_proj):
            scored.append(to_score.pop(0)[0])
        if i == last_proj:
            scored += gives.get(order[-1], [])
        steps += [("scores", g) for g in scored]
        while to_turn and to_turn[0][1] + scores_to_turn <= i and len(to_multiply) + len(halves(to_turn[0][0])) <= 2:
            g, _ = to_turn.pop(0)
            for c in halves(g):
                steps.append(("turn", g, c))
                to_multiply.append((g, c, i))
        to_turn += [(g, i) for g in scored]
        steps += [("exp", g) for g in scored]
        steps += [("lo", name) for name in to_lo] if last else []
        if not last and piece[2] == 1:
            name = piece[1]
            finished[name] = i
            if i < last_proj:
                to_score += [(g, i) for g in gives.get(name, [])]
            steps.append(("hi", name))
        steps += [("lo", name) for name in to_lo] if not last else []
        to_lo = [piece[1]] if not last and piece[2] == 1 else []
        steps += [("probs", g) for g in scored]
    assert not (to_score or to_turn or to_multiply or to_cat), (to_score, to_turn, to_multiply, to_cat)
    return steps + [("outs", *OUT_ORDER[2:])]


FF_CHUNKS = 22


def plan_ffn():
    units = [("w13", 0), ("w13", 1)]
    for s in range(1, FF_CHUNKS // 2):
        units += [("w13", 2 * s), ("w13", 2 * s + 1), ("w2", s - 1)]
    return units + [("w2", FF_CHUNKS // 2 - 1)]


FFN_HEAD = 5
FFN_TURNS = 4


def build(nc, x_in, mem_in, w13_in, w2_in, ln_g, ln_b, w_mem_kv, w_out, a_w_in, lambdas, subln_g,
          b_w_in, b_sink, out):
    depth, dm, ff2 = w13_in[0].shape
    ff = ff2 // 2
    seq = x_in.shape[1]
    KT = dm // P
    TT = seq // P
    assert (KT, TT, ff) == (8, 2, FF_CHUNKS * P) and depth == 2
    alpha = (2 * depth) ** 0.25

    mixers = [plan_mixer("A"), plan_mixer("B")]
    kinds = ["A", "B"]

    units = []
    ffn_first_unit, mixer_unit = {}, {}
    for layer in range(depth):
        for half in range(2):
            ffn_first_unit[layer, half] = len(units)
            units += [(kind, layer, half, n) for kind, n in plan_ffn()]
            if half == 0:
                for step in mixers[layer]:
                    for name in unit_names(step):
                        mixer_unit[layer, name] = len(units)
                        units.append(("proj" if step[0] == "proj" else "out", layer, name, 0))
    dmas_of = lambda unit: {"w13": 2, "w2": 1, "out": 1}.get(
        unit[0], 4 if unit[1] == 1 and unit[2] in ("q0", "q1", "q2") else
        2 if unit[1] == 0 and str(unit[2]).startswith("qk") else 1)
    landed_at, total = [], [0] * RING
    for n, unit in enumerate(units):
        total[n % RING] += 16 * dmas_of(unit)
        landed_at.append(total[n % RING])
    n_units = len(units)
    last_unit = [n for n, unit in enumerate(units) if unit[0] == "w2" and unit[3] == FF_CHUNKS // 2 - 1
                 or unit[0] == "out" and unit[2] == OUT_ORDER[3]]

    proj_of, n_proj = {}, 0
    ffn_first_proj, projections, cat_needs = {}, [], {}
    job_of, n_jobs = {}, 0

    def new_job(key):
        nonlocal n_jobs
        job_of[key] = n_jobs
        n_jobs += 1

    for key in [("x", -1, t, h) for t in range(TT) for h in range(2)] + [("mem", t, h) for t in range(TT) for h in range(2)]:
        new_job(key)
    cat_of = {}
    values_count, n_values = {}, 0
    rms_count, n_rms = {}, 0
    scores_count, n_scores = {}, 0
    act_copies, dve_copies = {}, {}
    for layer in range(depth):
        for half in range(2):
            ffn_first_proj[layer, half] = n_proj
            n_proj += FF_CHUNKS
            projections += [("chunk", FF_CHUNKS * (2 * layer + half) + f) for f in range(FF_CHUNKS)]
            norm = 3 * layer + 2 * half
            if norm < 3 * depth - 1:
                for t in range(TT):
                    for h in range(2):
                        new_job(("x", norm, t, h))
            if half == 0:
                for step in mixers[layer]:
                    if step[0] == "proj" and step[2] == 0:
                        proj_of[layer, step[1]] = n_proj
                        n_proj += 1
                        projections.append(("mixer", (layer, step[1])))
                        if step[1] == "mem_v" or step[1][0] == "v":
                            dve_copies[layer, step[1]] = len(dve_copies) + 1
                        else:
                            act_copies[layer, step[1]] = len(act_copies) + 1
                    elif step[0] == "scores":
                        scores_count[layer, step[1]] = n_scores
                        n_scores += 1
                    elif step[0] == "turn":
                        new_job((layer, *step[1:]))
                        values_count[layer, step[1], step[2]] = n_values
                        n_values += 1
                        if kinds[layer] == "A" and step[1] >= 2:
                            rms_count[layer, step[1]] = n_rms
                            n_rms += 1
                    elif step[0] == "cat":
                        cat_of[layer, step[1]] = (n_proj, len(cat_of))
                        projections.append(("cat", len(cat_of) - 1))
                        n_proj += 1
                        heads_jobs = [j for key, j in job_of.items() if len(key) == 3 and key[0] == layer
                                      and key[1] in head_groups(kinds[layer], step[1])]
                        cat_needs[layer, step[1]] = [max(j for j in heads_jobs if j % 2 == b)
                                                     for b in range(2) if any(j % 2 == b for j in heads_jobs)]
                for t in range(TT):
                    for h in range(2):
                        new_job(("x", 3 * layer + 1, t, h))

    ctx = ExitStack()
    with ctx:
        def sb(name, shape, dt=F32):
            return ctx.enter_context(nc.sbuf_tensor(name, shape, dt))

        def sem(name):
            return ctx.enter_context(nc.semaphore(name))

        raw = [sb(f"raw{i}", [P, UNIT]) for i in range(RING)]
        w_hi = [sb(f"w_hi{i}", [P, UNIT], F32R) for i in range(RING)]
        w_lo = [sb(f"w_lo{i}", [P, UNIT], F32R) for i in range(RING)]
        x = sb("x", [P, TT, dm])
        x_t_hi = sb("x_t_hi", [P, KT, seq], F32R)
        x_t_lo = sb("x_t_lo", [P, KT, seq], F32R)
        mem_t_hi = sb("mem_t_hi", [P, KT, seq], F32R)
        mem_t_lo = sb("mem_t_lo", [P, KT, seq], F32R)
        act_hi = sb("act_hi", [P, KT, seq], F32R)
        act_lo = sb("act_lo", [P, KT, seq], F32R)
        wide = sb("wide", [P, TT, dm])
        gain = [sb(f"gain{i}", [P, 2, dm]) for i in range(2)]
        silu = sb("silu", [P, 2, seq])
        gated = sb("gated", [P, 2, seq])
        q_k = sb("q_k", [P, 2, 2, seq])
        k_win = sb("k_win", [P, 2, seq])
        k_mem = sb("k_mem", [P, 2, seq])
        q_mem = sb("q_mem", [P, 2, seq])
        v_tok = sb("v_tok", [P, TT, DIFF_HEADS * P])
        v_mem = sb("v_mem", [P, TT, 4 * HEAD])
        probs = sb("probs", [P, PROBS, 2, TT, seq])
        probs_t = sb("probs_t", [P, 2, TT, seq])
        ident = sb("ident", [P, P])
        minus_dist = sb("minus_dist", [P, TT, seq])
        minus_dist_win = sb("minus_dist_win", [P, TT, seq])
        squares = sb("squares", [P, 2, TT, P])
        bn = sb("bn", [P, 2, 6])
        mean_var = sb("mean_var", [P, TT, 2])
        var_eps = sb("var_eps", [P, TT])
        rstd = sb("rstd", [P, TT])
        minus_half = sb("minus_half", [P, TT])
        minus_max = sb("minus_max", [P, PROBS, 2, TT])
        sums = sb("sums", [P, PROBS, 2, TT])
        sink_exp = sb("sink_exp", [P, PROBS, 2, TT])
        inv = sb("inv", [P, PROBS, 2, TT])
        rms_sq = sb("rms_sq", [P, 2, TT])
        rms_eps = sb("rms_eps", [P, 2, TT])
        rms = sb("rms", [P, 2, TT])
        sink = sb("sink", [P, WIN_HEADS])
        minus_sink = sb("minus_sink", [P, WIN_HEADS])
        sub_gain = sb("sub_gain", [P, P])
        lam_in = sb("lam_in", [P, 4, HEAD])
        lam_prod = sb("lam_prod", [P, 2, HEAD])
        lam_dot = sb("lam_dot", [P, 2])
        lam_exp = sb("lam_exp", [P, 2])
        minus_lam = sb("minus_lam", [P, 1])

        Y = ctx.enter_context(nc.psum_tensor("Y", [P, TT, dm], F32))
        G = ctx.enter_context(nc.psum_tensor("G", [P, 2, 2, seq], F32))
        T = ctx.enter_context(nc.psum_tensor("T", [P, 2, 512], F32))

        raw_landed = [sem(f"raw_landed{i}") for i in range(RING)]
        hi_made = sem("hi_made")
        lo_made = sem("lo_made")
        unit_used = sem("unit_used")
        silu_made = sem("silu_made")
        gate_steps = sem("gate_steps")
        y_full = sem("y_full")
        turn_full = sem("turn_full")
        turn_copied = sem("turn_copied")
        turn_free = [sem(f"turn_free{i}") for i in range(2)]
        scores_full = sem("scores_full")
        scores_free = sem("scores_free")
        max_made = sem("max_made")
        exp_made = sem("exp_made")
        probs_made = sem("probs_made")
        values_full = sem("values_full")
        squares_made = sem("squares_made")
        rms_made = sem("rms_made")
        cat_full = sem("cat_full")
        cat_hi_made = sem("cat_hi_made")
        cat_made = sem("cat_made")
        act_copied = sem("act_copied")
        dve_copied = sem("dve_copied")
        y_read = sem("y_read")
        var_made = sem("var_made")
        rstd_made = sem("rstd_made")
        x_made = sem("x_made")
        gain_landed = [sem(f"gain_landed{i}") for i in range(2)]
        x_landed = sem("x_landed")
        mem_landed = sem("mem_landed")
        small_landed = sem("small_landed")
        ident_made = sem("ident_made")
        dist_made = sem("dist_made")
        lam_dotted = sem("lam_dotted")
        lam_exped = sem("lam_exped")
        dve_done = sem("dve_done")
        pool_done = sem("pool_done")
        out_landed = sem("out_landed")

        block = ctx.enter_context(nc.Block())

        def at(value, per_turn, turn):
            return value if turn is None else value + turn * per_turn

        FFN_UNIT_STEP = 6

        def norm_after_ffn(layer, half):
            return 3 * layer + 2 * half

        @block.sync
        def _(sp):
            def load(u, turn=None):
                kind, layer, which, n = units[u]
                dst = raw[u % RING]
                done = raw_landed[u % RING]
                if u >= RING:
                    sp.wait_ge(lo_made, at(u - RING + 1, FFN_UNIT_STEP, turn))
                if kind == "w13":
                    src = w13_in[which][layer].rearrange("(k p) n -> p k n", p=P)
                    to = dst[:, :].rearrange("p (k g n) -> p g k n", k=KT, g=2)
                    for g in range(2):
                        col = at(g * ff + n * P, 4 * P, turn)
                        sp.dma_start(to[:, g], src[:, :, bass.ds(col, P)]).then_inc(done, 16)
                elif kind in ("w2", "out"):
                    w = w2_in[which][layer] if kind == "w2" else w_out[layer]
                    pair = n if kind == "w2" else which
                    src = w.rearrange("(m p) n -> p m n", p=P)
                    to = dst[:, :].rearrange("p (m n) -> p m n", m=2)
                    sp.dma_start(to, src[:, bass.ds(at(2 * pair, 4, turn), 2), :]).then_inc(done, 16)
                else:
                    name = which
                    if name in ("mem_k", "mem_v"):
                        w, cols = w_mem_kv[layer], [(4 * HEAD if name == "mem_v" else 0, 4 * HEAD)]
                    elif layer == 0:
                        w = a_w_in[0]
                        width = DIFF_HEADS * P
                        if name == "q_mem":
                            cols = [(3 * width, 256)]
                        elif name[0] == "v":
                            cols = [(2 * width + 256 * int(name[1]), 256)]
                        else:
                            cols = [(P * int(name[2]), P), (width + P * int(name[2]), P)]
                    else:
                        w = b_w_in[0]
                        width = WIN_HEADS * HEAD
                        if name == "q_mem":
                            cols = [(width + 512, 256)]
                        elif name == "k":
                            cols = [(width, 256)]
                        elif name == "v":
                            cols = [(width + 256, 256)]
                        else:
                            heads = [h for g in (2 * int(name[1]), 2 * int(name[1]) + 1) for h in window_heads(g)]
                            cols = [(h * HEAD, HEAD) for h in heads]
                    src = w.rearrange("(k p) n -> p k n", p=P)
                    to = dst[:, :].rearrange("p (k n) -> p k n", k=KT)
                    at_col = 0
                    for col, width in cols:
                        sp.dma_start(to[:, :, at_col:at_col + width], src[:, :, col:col + width]).then_inc(done, 16)
                        at_col += width

            for layer in range(depth):
                for half in range(2):
                    u0 = ffn_first_unit[layer, half]
                    for j in range(FFN_HEAD):
                        load(u0 + j)
                    with sp.Fori(0, FFN_TURNS) as turn:
                        for j in range(6):
                            load(u0 + FFN_HEAD + j, turn)
                    for j in range(FFN_HEAD + 6 * FFN_TURNS, 33):
                        load(u0 + j)
                    if half == 0:
                        for step in mixers[layer]:
                            for name in unit_names(step):
                                load(mixer_unit[layer, name])
            norm = 3 * depth - 1
            for t in range(TT):
                for h in range(2):
                    sp.wait_ge(x_made, 4 * norm + 2 * t + h + 1)
                    sp.dma_start(out[0, t * P:(t + 1) * P, h * 512:(h + 1) * 512],
                                 x[:, t, h * 512:(h + 1) * 512]).then_inc(out_landed, 16)
            sp.wait_ge(out_landed, 16 * 2 * TT)

        @block.gpsimd
        def _(pool):
            count = [0]

            def link(ins):
                count[0] += 1
                ins.then_inc(pool_done, 1)
                pool.wait_ge(pool_done, count[0])

            link(pool.memset(ident[:, :], 0.0))
            pool.affine_select(out=ident[:, :], in_=ident[:, :], compare_op=ALU.not_equal, fill=1.0,
                               base=0, pattern=[[-1, P]], channel_multiplier=1).then_inc(ident_made, 1)
            pool.iota(minus_dist[:, :, :], [[P, TT], [-1, seq]], base=0, channel_multiplier=1,
                      allow_small_or_imprecise_dtypes=True).then_inc(dist_made, 1)
            link(pool.memset(minus_half[:, :], -0.5))

            def norm_rstd(norm):
                for t in range(TT):
                    pool.wait_ge(var_made, TT * norm + t + 1)
                    pool.tensor_tensor(rstd[:, t:t + 1], var_eps[:, t:t + 1], minus_half[:, 0:1],
                                       ALU.pow).then_inc(rstd_made, 1)

            for layer in range(depth):
                norm_rstd(3 * layer)
                for step in mixers[layer]:
                    if step[0] == "values" and (layer, step[1]) in rms_count:
                        n = rms_count[layer, step[1]]
                        pool.wait_ge(squares_made, 2 * n + 2)
                        link(pool.tensor_scalar(rms_eps[:, n % 2], rms_sq[:, n % 2], 1.0 / P, LN_EPS,
                                                ALU.mult, ALU.add))
                        pool.tensor_tensor(rms[:, n % 2], rms_eps[:, n % 2], minus_half[:, :],
                                           ALU.pow).then_inc(rms_made, 1)
                norm_rstd(3 * layer + 1)
                norm_rstd(3 * layer + 2)

        @block.scalar
        def _(act):
            def load_gain(norm):
                i, layer = norm % 3, norm // 3
                buf = norm % 2
                for j, src in enumerate((ln_g[i], ln_b[i])):
                    act.dma_start(gain[buf][:, j, :], src[layer:layer + 1, :].to_broadcast([P, dm]))\
                       .then_inc(gain_landed[buf], 16)

            def split_hi(u, turn=None):
                if u >= n_units:
                    return
                per = 16 * 2 * dmas_of(units[u])
                act.wait_ge(raw_landed[u % RING], at(landed_at[u], per, turn))
                if u >= RING:
                    act.wait_ge(unit_used, at(u - RING + 1, FFN_UNIT_STEP, turn))
                act.activation(w_hi[u % RING][:, :], raw[u % RING][:, :], ACT.Copy).then_inc(hi_made, 1)

            def copy_turned(job, dst, shape=None):
                act.wait_ge(turn_full, job + 1)
                src = T[:, job % 2, :]
                if shape:
                    src = src.rearrange("p (a b) -> p a b", a=shape)
                act.activation(dst, src, ACT.Copy).then_inc(turn_copied, 1)

            def ffn(layer, half):
                u0, p0 = ffn_first_unit[layer, half], ffn_first_proj[layer, half]
                plan = plan_ffn()

                def after(j, turn=None):
                    kind, n = plan[j]
                    if kind == "w13":
                        p = p0 + n
                        act.wait_ge(unit_used, at(u0 + j + 1, FFN_UNIT_STEP, turn))
                        act.activation(silu[:, p % 2, :], G[:, p % 2, 0, :], ACT.Silu).then_inc(silu_made, 1)
                    split_hi(u0 + j + RING, turn)

                for j in range(FFN_HEAD):
                    after(j)
                if (layer, half) == (0, 0):
                    for t in range(TT):
                        for h in range(2):
                            copy_turned(job_of["mem", t, h], mem_t_hi[:, 4 * h:4 * h + 4, t * P:(t + 1) * P], 4)
                with act.Fori(0, FFN_TURNS) as turn:
                    for j in range(FFN_HEAD, FFN_HEAD + 6):
                        after(j, turn)
                for j in range(FFN_HEAD + 6 * FFN_TURNS, 31):
                    after(j)

            def norm(n):
                if n < 3 * depth - 1:
                    if n % 3 == 0:
                        split_hi(last_unit[n] + RING - 1)
                        split_hi(last_unit[n] + RING)
                    for t in range(TT):
                        if n % 3:
                            split_hi(last_unit[n] + RING - 1 + t)
                        for h in range(2):
                            copy_turned(job_of["x", n, t, h],
                                        x_t_hi[:, 4 * h:4 * h + 4, t * P:(t + 1) * P], 4)
                    if n + 2 < 3 * depth:
                        load_gain_after = x_made
                        act.wait_ge(load_gain_after, 4 * (n + 1))
                        load_gain(n + 2)

            def mixer(layer):
                if kinds[layer] == "A":
                    act.wait_ge(lam_dotted, 1)
                    act.activation(lam_exp[:, :], lam_dot[:, :], ACT.Exp).then_inc(lam_exped, 1)
                for step in mixers[layer]:
                    if step[0] == "proj" and step[2] == 1:
                        name = step[1]
                        u, p = mixer_unit[layer, name], proj_of[layer, name]
                        if (layer, name) in act_copies:
                            act.wait_ge(unit_used, u + 1)
                            bank = G[:, p % 2, :, :]
                            scale = HEAD ** -0.5
                            if name == "mem_k":
                                last = act.activation(k_mem[:, :, :], bank, ACT.Copy)
                            elif name == "q_mem":
                                last = act.activation(q_mem[:, :, :], bank, ACT.Copy, scale=scale)
                            elif name == "k":
                                last = act.activation(k_win[:, :, :], bank, ACT.Copy)
                            elif kinds[layer] == "B":
                                j = int(name[1])
                                if j >= 2:
                                    act.wait_ge(scores_full, scores_count[layer, 2 + 2 * (j - 2) + 1] + 1)
                                last = act.activation(q_k[:, j % 2, :, :], bank, ACT.Copy, scale=scale)
                            else:
                                h = int(name[2])
                                if h >= 2:
                                    act.wait_ge(scores_full, scores_count[layer, 2 + h - 2] + 1)
                                act.activation(q_k[:, h % 2, 0, :], bank[:, 0, :], ACT.Copy, scale=scale)
                                last = act.activation(q_k[:, h % 2, 1, :], bank[:, 1, :], ACT.Copy)
                            last.then_inc(act_copied, 1)
                    elif step[0] == "hi":
                        split_hi(mixer_unit[layer, step[1]] + RING)
                    elif step[0] == "exp":
                        g = step[1]
                        n = scores_count[layer, g]
                        b = n % PROBS
                        act.wait_ge(max_made, n + 1)
                        for c in range(2):
                            for t in range(TT):
                                last = act.activation(probs[:, b, c, t, :], probs[:, b, c, t, :], ACT.Exp,
                                                      bias=minus_max[:, b, c, t:t + 1],
                                                      accum_out=sums[:, b, c, t:t + 1])
                            if kinds[layer] == "B" and g >= 2:
                                h = window_heads(g - 2)[c]
                                last = act.activation(sink_exp[:, b, c, :], minus_max[:, b, c, :], ACT.Exp,
                                                      bias=sink[:, h:h + 1])
                        last.then_inc(exp_made, 1)
                    elif step[0] == "turn":
                        job = job_of[layer, step[1], step[2]]
                        n = values_count[layer, step[1], step[2]]
                        copy_turned(job, probs_t[:, n % 2].rearrange("p a b -> p (a b)"))
                    elif step[0] == "values":
                        if (layer, step[1]) in rms_count:
                            n = rms_count[layer, step[1]]
                            job = job_of[layer, step[1], step[2]]
                            act.wait_ge(values_full, values_count[layer, step[1], step[2]] + 1)
                            if n >= 2:
                                act.wait_ge(rms_made, n - 1)
                            for t in range(TT):
                                act.activation(squares[:, n % 2, t, :], T[:, job % 2, t * P:(t + 1) * P], ACT.Square,
                                               accum_out=rms_sq[:, n % 2, t:t + 1]).then_inc(squares_made, 1)
                    elif step[0] == "cat":
                        kp = step[1]
                        p, c = cat_of[layer, kp]
                        act.wait_ge(cat_full, c + 1)
                        act.activation(act_hi[:, 2 * kp:2 * kp + 2, :], G[:, p % 2, :, :],
                                       ACT.Copy).then_inc(cat_hi_made, 1)

            for t in range(TT):
                act.dma_start(x[:, t, :], x_in[0, t * P:(t + 1) * P, :]).then_inc(x_landed, 16)
            for t in range(TT):
                for h in range(2):
                    copy_turned(job_of["x", -1, t, h], x_t_hi[:, 4 * h:4 * h + 4, t * P:(t + 1) * P], 4)
            for u in range(RING):
                split_hi(u)
            for t in range(TT):
                act.dma_start(wide[:, t, :], mem_in[0, t * P:(t + 1) * P, :]).then_inc(mem_landed, 16)
            for i, v in enumerate(lambdas):
                act.dma_start(lam_in[:, i, :], v[0:1, :].to_broadcast([P, HEAD])).then_inc(small_landed, 16)
            act.dma_start(sub_gain[:, :], subln_g[0:1, :].to_broadcast([P, P])).then_inc(small_landed, 16)
            act.dma_start(sink[:, :], b_sink[0:1, :].to_broadcast([P, WIN_HEADS])).then_inc(small_landed, 16)
            load_gain(0)
            load_gain(1)
            for layer in range(depth):
                ffn(layer, 0)
                norm(3 * layer)
                mixer(layer)
                norm(3 * layer + 1)
                ffn(layer, 1)
                norm(3 * layer + 2)

        @block.vector
        def _(dve):
            count = [0]

            def link(ins):
                count[0] += 1
                ins.then_inc(dve_done, 1)
                dve.wait_ge(dve_done, count[0])

            def split_lo(u, turn=None):
                if u >= n_units:
                    return
                dve.wait_ge(hi_made, at(u + 1, FFN_UNIT_STEP, turn))
                dve.tensor_tensor(w_lo[u % RING][:, :], raw[u % RING][:, :],
                                  w_hi[u % RING][:, :].bitcast(F32), ALU.subtract).then_inc(lo_made, 1)

            def turned_lo(job, hi, lo, shape=None):
                dve.wait_ge(turn_copied, job + 1)
                src = T[:, job % 2, :]
                if shape:
                    src = src.rearrange("p (a b) -> p a b", a=shape)
                dve.tensor_tensor(lo, src, hi.bitcast(F32), ALU.subtract).then_inc(turn_free[job % 2], 1)

            def x_turned_lo(key, hi, lo):
                _, t, h = key[-3:]
                part = (slice(None), slice(4 * h, 4 * h + 4), slice(t * P, (t + 1) * P))
                turned_lo(job_of[key], hi[part], lo[part], 4)

            def ffn(layer, half):
                u0, p0 = ffn_first_unit[layer, half], ffn_first_proj[layer, half]
                chunk0 = FF_CHUNKS * (2 * layer + half)
                plan = plan_ffn()

                def after(j, turn=None):
                    kind, n = plan[j]
                    if kind == "w13":
                        b, slot, c = (p0 + n) % 2, n % 4, chunk0 + n
                        dve.wait_ge(silu_made, at(c + 1, 4, turn))
                        dve.tensor_tensor(gated[:, b, :], silu[:, b, :], G[:, b, 1, :], ALU.mult)\
                           .then_inc(gate_steps, 1)
                        dve.wait_ge(gate_steps, at(3 * c + 1, 12, turn))
                        dve.tensor_copy(act_hi[:, slot, :], gated[:, b, :]).then_inc(gate_steps, 1)
                        dve.wait_ge(gate_steps, at(3 * c + 2, 12, turn))
                        dve.tensor_tensor(act_lo[:, slot, :], gated[:, b, :], act_hi[:, slot, :].bitcast(F32),
                                          ALU.subtract).then_inc(gate_steps, 1)
                    split_lo(u0 + j + RING, turn)

                for j in range(FFN_HEAD):
                    after(j)
                if (layer, half) == (0, 0):
                    for t in range(TT):
                        for h in range(2):
                            x_turned_lo(("mem", t, h), mem_t_hi, mem_t_lo)
                with dve.Fori(0, FFN_TURNS) as turn:
                    for j in range(FFN_HEAD, FFN_HEAD + 6):
                        after(j, turn)
                for j in range(FFN_HEAD + 6 * FFN_TURNS, 31):
                    after(j)

            def norm(n):
                c = (1.0 if n % 3 == 1 else 0.5) / alpha
                g = gain[n % 2]
                dve.wait_ge(gain_landed[n % 2], 32 * (n // 2 + 1))
                for t in range(TT):
                    if t == 0:
                        dve.wait_ge(y_full, n + 1)
                    else:
                        dve.wait_ge(unit_used, last_unit[n] + 1)
                    dve.scalar_tensor_tensor(out=wide[:, t, :], in0=Y[:, t, :], scalar=c, in1=x[:, t, :],
                                             op0=ALU.mult, op1=ALU.add).then_inc(y_read, 1)
                    dve.wait_ge(y_read, TT * n + t + 1)
                    for h in range(2):
                        last = dve.bn_stats(bn[:, h, :], wide[:, t, h * 512:(h + 1) * 512])
                    link(last)
                    link(dve.bn_aggr(mean_var[:, t, :], bn[:, :, :].rearrange("p a b -> p (a b)")))
                    dve.tensor_scalar(var_eps[:, t:t + 1], mean_var[:, t, 1:2], LN_EPS / alpha ** 2, None,
                                      ALU.add).then_inc(var_made, 1)
                    link(dve.scalar_tensor_tensor(out=wide[:, t, :], in0=wide[:, t, :], scalar=mean_var[:, t, 0:1],
                                                  in1=g[:, 0, :], op0=ALU.subtract, op1=ALU.mult))
                    dve.wait_ge(rstd_made, TT * n + t + 1)
                    for h in range(2):
                        part = slice(h * 512, (h + 1) * 512)
                        dve.scalar_tensor_tensor(out=x[:, t, part], in0=wide[:, t, part], scalar=rstd[:, t:t + 1],
                                                 in1=g[:, 1, part], op0=ALU.mult, op1=ALU.add).then_inc(x_made, 1)
                    if n % 3 == 0:
                        split_lo(last_unit[n] + RING - 1 + t)
                if n < 3 * depth - 1:
                    for t in range(TT):
                        for h in range(2):
                            x_turned_lo(("x", n, t, h), x_t_hi, x_t_lo)
                if n % 3:
                    split_lo(last_unit[n] + RING - 1)
                    split_lo(last_unit[n] + RING)

            def mixer(layer):
                a = kinds[layer] == "A"
                if a:
                    dve.wait_ge(small_landed, 16 * 6)
                    for i in range(2):
                        last = dve.tensor_tensor(lam_prod[:, i, :], lam_in[:, 2 * i, :], lam_in[:, 2 * i + 1, :], ALU.mult)
                    link(last)
                    dve.tensor_reduce(lam_dot[:, :], lam_prod[:, :, :], AX_X, ALU.add).then_inc(lam_dotted, 1)
                    dve.tensor_scalar(minus_sink[:, :], sink[:, :], -1.0, None, ALU.mult)
                    link(dve.tensor_scalar(sub_gain[:, :], sub_gain[:, :], 1.0 - LAM_INIT, None, ALU.mult))
                    dve.wait_ge(lam_exped, 1)
                    link(dve.tensor_tensor(minus_lam[:, :], lam_exp[:, 1:2], lam_exp[:, 0:1], ALU.subtract))
                    link(dve.tensor_scalar(minus_lam[:, :], minus_lam[:, :], -LAM_INIT, None, ALU.add))
                for step in mixers[layer]:
                    if step[0] == "proj" and step[2] == 1:
                        name = step[1]
                        u, p = mixer_unit[layer, name], proj_of[layer, name]
                        if (layer, name) in dve_copies:
                            dve.wait_ge(unit_used, u + 1)
                            if name == "mem_v":
                                dst = v_mem[:, :, :]
                            elif a:
                                dst = v_tok[:, :, 256 * int(name[1]):256 * int(name[1]) + 256]
                            else:
                                dst = v_tok[:, :, 0:256]
                            dve.tensor_copy(dst, G[:, p % 2, :, :]).then_inc(dve_copied, 1)
                    elif step[0] == "lo":
                        split_lo(mixer_unit[layer, step[1]] + RING)
                    elif step[0] == "scores":
                        g = step[1]
                        n = scores_count[layer, g]
                        b = n % PROBS
                        dve.wait_ge(scores_full, n + 1)
                        if n >= PROBS:
                            g_before = [s for s, m in scores_count.items() if m == n - PROBS][0]
                            dve.wait_ge(turn_full, last_job_of(*g_before) + 1)
                        for c in range(2):
                            src = Y[:, n % 2, c * 512:(c + 1) * 512]
                            dst = probs[:, b, c].rearrange("p a b -> p (a b)")
                            if g < 2:
                                last = dve.tensor_copy(dst, src)
                            else:
                                s = slope(DIFF_HEADS, g - 2) if a else slope(WIN_HEADS, window_heads(g - 2)[c])
                                dist = (minus_dist if a else minus_dist_win)[:, :, :]
                                last = dve.scalar_tensor_tensor(
                                    out=dst, in0=dist.rearrange("p a b -> p (a b)"), scalar=s, in1=src,
                                    op0=ALU.mult, op1=ALU.add)
                        last.then_inc(scores_free, 1)
                        dve.wait_ge(scores_free, n + 1)
                        flat = minus_max[:, b].rearrange("p c t -> p (c t)")
                        top = dve.tensor_reduce(flat, probs[:, b].rearrange("p c t k -> p (c t) k"), AX_X,
                                                ALU.max, negate=True)
                        if not a and g >= 2:
                            link(top)
                            for c in range(2):
                                h = window_heads(g - 2)[c]
                                top = dve.tensor_scalar(minus_max[:, b, c, :], minus_max[:, b, c, :],
                                                        minus_sink[:, h:h + 1], None, ALU.min)
                        top.then_inc(max_made, 1)
                    elif step[0] == "probs":
                        g = step[1]
                        n = scores_count[layer, g]
                        b = n % PROBS
                        dve.wait_ge(exp_made, n + 1)
                        flat = lambda s: s[:, b].rearrange("p c t -> p (c t)")
                        if not a and g >= 2:
                            link(dve.tensor_tensor(flat(sums), flat(sums), flat(sink_exp), ALU.add))
                        if not a or g < 2:
                            dve.reciprocal(flat(inv), flat(sums)).then_inc(probs_made, 1)
                            continue
                        link(dve.reciprocal(flat(inv), flat(sums)))
                        link(dve.tensor_scalar(inv[:, b, 1, :], inv[:, b, 1, :], minus_lam[:, 0:1], None, ALU.mult))
                        for t in range(TT):
                            last = dve.tensor_scalar(probs[:, b, 1, t, :], probs[:, b, 1, t, :],
                                                     inv[:, b, 1, t:t + 1], None, ALU.mult)
                        link(last)
                        for t in range(TT):
                            last = dve.scalar_tensor_tensor(
                                out=probs[:, b, 0, t, :], in0=probs[:, b, 0, t, :], scalar=inv[:, b, 0, t:t + 1],
                                in1=probs[:, b, 1, t, :], op0=ALU.mult, op1=ALU.add)
                        last.then_inc(probs_made, 1)
                    elif step[0] == "values":
                        g, c = step[1:]
                        job, n = job_of[layer, g, c], values_count[layer, g, c]
                        b = scores_count[layer, g] % PROBS
                        bank = T[:, job % 2, :]
                        if (layer, g) in rms_count:
                            r = rms_count[layer, g]
                            dve.wait_ge(rms_made, r + 1)
                            col = (g - 2) * P
                            for t in range(TT):
                                last = dve.scalar_tensor_tensor(
                                    out=wide[:, t, col:col + P], in0=bank[:, t * P:(t + 1) * P],
                                    scalar=rms[:, r % 2, t:t + 1], in1=sub_gain[:, :], op0=ALU.mult, op1=ALU.mult)
                        else:
                            dve.wait_ge(values_full, n + 1)
                            head = WIN_HEADS + 2 * g + c if g < 2 else window_heads(g - 2)[c]
                            for t in range(TT):
                                last = dve.tensor_scalar(
                                    wide[:, t, head * HEAD:(head + 1) * HEAD], bank[:, t * HEAD:(t + 1) * HEAD],
                                    inv[:, b, c, t:t + 1], None, ALU.mult)
                        last.then_inc(turn_free[job % 2], 1)
                    elif step[0] == "cat":
                        kp = step[1]
                        p, c = cat_of[layer, kp]
                        dve.wait_ge(cat_hi_made, c + 1)
                        dve.tensor_tensor(act_lo[:, 2 * kp:2 * kp + 2, :], G[:, p % 2, :, :],
                                          act_hi[:, 2 * kp:2 * kp + 2, :].bitcast(F32),
                                          ALU.subtract).then_inc(cat_made, 1)

            def last_job_of(layer, g):
                return max(j for key, j in job_of.items() if key[:2] == (layer, g) and len(key) == 3)

            dve.wait_ge(dist_made, 1)
            flat = lambda s: s[:, :, :].rearrange("p a b -> p (a b)")
            link(dve.scalar_tensor_tensor(out=flat(minus_dist), in0=flat(minus_dist), scalar=-1.0,
                                          in1=flat(minus_dist), op0=ALU.mult, op1=ALU.min))
            link(dve.tensor_scalar(flat(minus_dist_win), flat(minus_dist), -float(WINDOW), NEG,
                                   ALU.is_lt, ALU.mult))
            link(dve.tensor_tensor(flat(minus_dist_win), flat(minus_dist_win), flat(minus_dist), ALU.add))
            for t in range(TT):
                for h in range(2):
                    x_turned_lo(("x", -1, t, h), x_t_hi, x_t_lo)
            for u in range(RING):
                split_lo(u)
            for layer in range(depth):
                ffn(layer, 0)
                norm(3 * layer)
                mixer(layer)
                norm(3 * layer + 1)
                ffn(layer, 1)
                norm(3 * layer + 2)

        @block.tensor
        def _(pe):
            PASSES = [(0, 0), (0, 1), (1, 0)]

            def job_done(job):
                pe.wait_ge(turn_free[job % 2], job // 2 + 1)

            def start_job(job):
                if job >= 2:
                    job_done(job - 2)

            def turn_x(key, src):
                _, t, h = key[-3:]
                job = job_of[key]
                start_job(job)
                for k in range(4):
                    col = (4 * h + k) * P
                    last = pe.transpose(T[:, job % 2, k * P:(k + 1) * P], src[:, t, col:col + P], ident[:, :])
                last.then_inc(turn_full, 1)

            def wait_weights(u, turn=None):
                pe.wait_ge(lo_made, at(u + 1, FFN_UNIT_STEP, turn))

            def feature_major(u, p, src_hi, src_lo, parts=(0, 1)):
                moving = (src_hi, src_lo)
                view = [w[u % RING][:, :].rearrange("p (k g n) -> p k g n", k=KT, g=2) for w in (w_hi, w_lo)]
                for g in parts:
                    for k in range(KT):
                        for i, (wi, xi) in enumerate(PASSES):
                            last = pe.matmul(G[:, p % 2, g, :], view[wi][:, k, g, :], moving[xi][:, k, :],
                                             start=(k == 0 and i == 0), stop=(k == KT - 1 and i == 2))
                if 1 in parts:
                    last.then_inc(unit_used, 1)

            def token_major(u, p, src_hi, src_lo, parts):
                stationary = (src_hi, src_lo)
                view = [w[u % RING][:, :].rearrange("p (k n) -> p k n", k=KT) for w in (w_hi, w_lo)]
                for t in parts:
                    for k in range(KT):
                        for i, (wi, xi) in enumerate(PASSES):
                            last = pe.matmul(G[:, p % 2, t, :], stationary[xi][:, k, t * P:(t + 1) * P],
                                             view[wi][:, k, :], start=(k == 0 and i == 0),
                                             stop=(k == KT - 1 and i == 2))
                if 1 in parts:
                    last.then_inc(unit_used, 1)

            def accumulate(u, slots, t, first, stop, tiles=(0, 1)):
                view = [w[u % RING][:, :].rearrange("p (m n) -> p m n", m=2) for w in (w_hi, w_lo)]
                stationary = (act_hi, act_lo)
                for m in tiles:
                    for half in range(2):
                        cols = slice(half * 512, (half + 1) * 512)
                        for i, (wi, xi) in enumerate(PASSES):
                            last = pe.matmul(Y[:, t, cols], stationary[xi][:, slots[m], t * P:(t + 1) * P],
                                             view[wi][:, m, cols], start=(first and m == 0 and i == 0),
                                             stop=(stop and m == 1 and i == 2))
                return last

            def bank_free(p, turn=None):
                if p < 2:
                    return
                stage, which = projections[p - 2]
                if stage == "chunk":
                    pe.wait_ge(gate_steps, at(3 * which + 1, 12, turn))
                elif stage == "cat":
                    pe.wait_ge(cat_made, which + 1)
                elif which in act_copies:
                    pe.wait_ge(act_copied, act_copies[which])
                else:
                    pe.wait_ge(dve_copied, dve_copies[which])

            def ffn(layer, half, y_done):
                u0, p0 = ffn_first_unit[layer, half], ffn_first_proj[layer, half]
                chunk0 = FF_CHUNKS * (2 * layer + half)
                plan = plan_ffn()

                def unit(j, turn=None):
                    kind, n = plan[j]
                    u = u0 + j
                    wait_weights(u, turn)
                    if kind == "w13":
                        bank_free(p0 + n, turn)
                        feature_major(u, p0 + n, x_t_hi, x_t_lo)
                    else:
                        pe.wait_ge(gate_steps, at(3 * (chunk0 + 2 * n + 2), 12, turn))
                        slots = [(2 * n) % 4, (2 * n + 1) % 4]
                        if n == 0 and y_done:
                            pe.wait_ge(y_read, y_done)
                        for t in range(TT):
                            last = accumulate(u, slots, t, first=(turn is None and n == 0), stop=False)
                        last.then_inc(unit_used, 1)

                for j in range(FFN_HEAD):
                    unit(j)
                if (layer, half) == (0, 0):
                    pe.wait_ge(mem_landed, 16 * TT)
                    for t in range(TT):
                        for h in range(2):
                            turn_x(("mem", t, h), wide)
                with pe.Fori(0, FFN_TURNS) as turn:
                    for j in range(FFN_HEAD, FFN_HEAD + 6):
                        unit(j, turn)
                j = FFN_HEAD + 6 * FFN_TURNS
                unit(j)
                unit(j + 1)
                wait_weights(u0 + j + 2)
                pe.wait_ge(gate_steps, 3 * (chunk0 + FF_CHUNKS - 2))
                for t in range(TT):
                    last = accumulate(u0 + j + 2, [(FF_CHUNKS - 4) % 4, (FF_CHUNKS - 3) % 4], t, False, False)
                    if t == TT - 1:
                        last.then_inc(unit_used, 1)
                    if t == 0:
                        wait_weights(u0 + j + 3)
                        pe.wait_ge(gate_steps, 3 * (chunk0 + FF_CHUNKS))
                    last = accumulate(u0 + j + 3, [(FF_CHUNKS - 2) % 4, (FF_CHUNKS - 1) % 4], t, False, True)
                    last.then_inc(y_full if t == 0 else unit_used, 1)

            def turn_norm(n):
                for t in range(TT):
                    for h in range(2):
                        pe.wait_ge(x_made, 4 * n + 2 * t + h + 1)
                        turn_x(("x", n, t, h), x)

            def x_turned(n):
                job_done(job_of["x", n, 1, 0])
                job_done(job_of["x", n, 1, 1])

            def mixer(layer):
                a = kinds[layer] == "A"
                norm = 3 * layer
                for step in mixers[layer]:
                    if step[0] == "proj":
                        _, name, half = step
                        u, p = mixer_unit[layer, name], proj_of[layer, name]
                        if half == 0:
                            if name == "q_mem":
                                turn_norm(norm)
                                x_turned(norm)
                            wait_weights(u)
                            bank_free(p)
                        if name == "mem_k":
                            feature_major(u, p, mem_t_hi, mem_t_lo, (half,))
                        elif name == "mem_v":
                            token_major(u, p, mem_t_hi, mem_t_lo, (half,))
                        elif name[0] == "v":
                            token_major(u, p, x_t_hi, x_t_lo, (half,))
                        else:
                            feature_major(u, p, x_t_hi, x_t_lo, (half,))
                    elif step[0] == "scores":
                        g = step[1]
                        n = scores_count[layer, g]
                        b = n % 2
                        if g < 2:
                            pe.wait_ge(y_read, TT * (norm + 1))
                            pe.wait_ge(act_copied, act_copies[layer, "q_mem"])
                            q, k = q_mem[:, g, :], k_mem[:, g, :]
                        elif a:
                            pe.wait_ge(act_copied, act_copies[layer, f"qk{g - 2}"])
                            q, k = q_k[:, g % 2, 0, :], q_k[:, g % 2, 1, :]
                        else:
                            j = (g - 2) // 2
                            pe.wait_ge(act_copied, act_copies[layer, f"q{j}"])
                            q, k = q_k[:, j % 2, g % 2, :], k_win[:, (g - 2) // 3, :]
                        if n >= 2:
                            pe.wait_ge(scores_free, n - 1)
                        for t in range(TT):
                            for c in range(2):
                                rows = slice(c * HEAD, (c + 1) * HEAD)
                                last = pe.matmul(Y[:, b, c * 512 + t * seq:c * 512 + (t + 1) * seq],
                                                 q[rows, t * P:(t + 1) * P], k[rows, :], start=True, stop=True)
                        last.then_inc(scores_full, 1)
                    elif step[0] == "turn":
                        g, c = step[1:]
                        job = job_of[layer, g, c]
                        n = scores_count[layer, g]
                        pe.wait_ge(probs_made, n + 1)
                        start_job(job)
                        for kt in range(TT):
                            for t in range(TT):
                                at_col = kt * seq + t * P
                                last = pe.transpose(T[:, job % 2, at_col:at_col + P],
                                                    probs[:, n % PROBS, c, t, kt * P:(kt + 1) * P], ident[:, :])
                        last.then_inc(turn_full, 1)
                    elif step[0] == "values":
                        g, c = step[1:]
                        job, n = job_of[layer, g, c], values_count[layer, g, c]
                        pe.wait_ge(turn_copied, job + 1)
                        if g < 2:
                            pe.wait_ge(dve_copied, dve_copies[layer, "mem_v"])
                            v, width = v_mem[:, :, (2 * g + c) * HEAD:(2 * g + c + 1) * HEAD], HEAD
                        elif a:
                            h = g - 2
                            pe.wait_ge(dve_copied, dve_copies[layer, f"v{h // 2}"])
                            v, width = v_tok[:, :, h * P:(h + 1) * P], P
                        else:
                            kv = window_heads(g - 2)[c] // WIN_GROUP
                            pe.wait_ge(dve_copied, dve_copies[layer, "v"])
                            v, width = v_tok[:, :, kv * HEAD:(kv + 1) * HEAD], HEAD
                        for t in range(TT):
                            for kt in range(TT):
                                last = pe.matmul(T[:, job % 2, t * width:(t + 1) * width],
                                                 probs_t[:, n % 2, kt, t * P:(t + 1) * P], v[:, kt, :],
                                                 start=(kt == 0), stop=(kt == TT - 1))
                        last.then_inc(values_full, 1)
                    elif step[0] == "cat":
                        kp = step[1]
                        p, _ = cat_of[layer, kp]
                        for job_before in cat_needs[layer, kp]:
                            job_done(job_before)
                        bank_free(p)
                        for m in range(2):
                            for t in range(TT):
                                col = (2 * kp + m) * P
                                last = pe.transpose(G[:, p % 2, m, t * P:(t + 1) * P],
                                                    wide[:, t, col:col + P], ident[:, :])
                        last.then_inc(cat_full, 1)
                    elif step[0] == "out":
                        _, kp, t = step
                        u = mixer_unit[layer, kp]
                        first = kp == OUT_ORDER[0]
                        if t == 0:
                            wait_weights(u)
                            pe.wait_ge(cat_made, cat_of[layer, kp][1] + 1)
                        if first:
                            pe.wait_ge(scores_free, max(m for (l, _), m in scores_count.items()
                                                        if l == layer and m % 2 == t) + 1)
                        last = accumulate(u, [2 * kp, 2 * kp + 1], t, first, False)
                        if t == 1:
                            last.then_inc(unit_used, 1)
                    elif step[0] == "outs":
                        for t in range(TT):
                            for kp in step[1:]:
                                u = mixer_unit[layer, kp]
                                if t == 0:
                                    wait_weights(u)
                                    pe.wait_ge(cat_made, cat_of[layer, kp][1] + 1)
                                is_last = kp == step[2]
                                last = accumulate(u, [2 * kp, 2 * kp + 1], t, False, is_last)
                                if t == 0 and is_last:
                                    last.then_inc(y_full, 1)
                                elif t == 1:
                                    last.then_inc(unit_used, 1)

            pe.wait_ge(ident_made, 1)
            pe.wait_ge(x_landed, 16 * TT)
            for t in range(TT):
                for h in range(2):
                    turn_x(("x", -1, t, h), x)
            x_turned(-1)
            for layer in range(depth):
                ffn(layer, 0, TT * 3 * layer)
                mixer(layer)
                turn_norm(3 * layer + 1)
                x_turned(3 * layer + 1)
                ffn(layer, 1, TT * (3 * layer + 2))
                if layer < depth - 1:
                    turn_norm(3 * layer + 2)
                    x_turned(3 * layer + 2)


def window_heads(g):
    first = g % 3 + 6 * (g // 3)
    return first, first + WIN_GROUP


_INS = ["x", "mem", "ffn1_w13", "ffn1_w2", "ln1_g", "ln1_b", "w_mem_kv", "w_out", "ln2_g", "ln2_b",
        "ffn2_w13", "ffn2_w2", "ln3_g", "ln3_b", "a_w_in", "a_lambda_q1", "a_lambda_k1", "a_lambda_q2",
        "a_lambda_k2", "a_subln_g", "b_w_in", "b_sink"]


def kernel(**inputs):
    import numpy as _np
    import concourse.bacc as _bacc
    from concourse.bass_utils import run_bass_kernel_spmd as _run

    nc = _bacc.Bacc("TRN2", target_bir_lowering=False, num_devices=1)
    arrays, a = {}, {}
    for name in _INS:
        v = _np.ascontiguousarray(inputs[name])
        arrays[f"in_{name}"] = v
        a[name] = nc.dram_tensor(f"in_{name}", v.shape, mybir.dt.from_np(v.dtype), kind="ExternalInput").ap()
    out = nc.dram_tensor("out", arrays["in_x"].shape, F32, kind="ExternalOutput").ap()
    build(nc, a["x"], a["mem"], [a["ffn1_w13"], a["ffn2_w13"]], [a["ffn1_w2"], a["ffn2_w2"]],
          [a["ln1_g"], a["ln2_g"], a["ln3_g"]], [a["ln1_b"], a["ln2_b"], a["ln3_b"]], a["w_mem_kv"],
          a["w_out"], a["a_w_in"], [a["a_lambda_q1"], a["a_lambda_k1"], a["a_lambda_q2"], a["a_lambda_k2"]],
          a["a_subln_g"], a["b_w_in"], a["b_sink"], out)
    r = _run(nc, [arrays], core_ids=[0])
    return r.results[0]["out"]
```

```python
import math
from contextlib import ExitStack
from functools import partial

import concourse.bass as bass
from concourse import mybir

F32 = mybir.dt.float32
F32R = mybir.dt.float32r
ALU = mybir.AluOpType
ACT = mybir.ActivationFunctionType
AX_X = mybir.AxisListType.X

P = 128
RING = 3
UNIT = 2048
HEAD = 64
NEG = -1e30
LN_EPS = 1e-5

DIFF_HEADS = 6
WIN_HEADS = 12
WIN_GROUP = 3
WINDOW = 128
OUT_ORDER = [3, 0, 1, 2]
PROBS = 4
KEEP_BUSY = 20
LAM_INIT = 0.8 - 0.6 * math.exp(-0.3 * 0)


def slope(n_heads, head):
    return float(2.0 ** (-8.0 * (head + 1) / n_heads))



def head_groups(kind, pair):
    if pair == 3:
        return {0, 1}
    if kind == "A":
        return {2 + 2 * pair, 3 + 2 * pair}
    heads = range(4 * pair, 4 * pair + 4)
    return {2 + g for g in range(6) if set(window_heads(g)) & set(heads)}


def unit_names(step):
    if step[0] == "outs":
        return step[1:]
    return step[1:2] if step[0] in ("proj", "out") and step[2] == 0 else ()


def plan_mixer(kind):
    if kind == "A":
        order = ["mem_k", "mem_v", "q_mem", "qk0", "qk1", "v0", "qk2", "qk3", "v1", "qk4", "qk5", "v2"]
        gives = {"q_mem": [0, 1]} | {f"qk{h}": [2 + h] for h in range(6)}
        values_of = lambda g: "mem_v" if g < 2 else f"v{(g - 2) // 2}"
        scores_to_turn = 2
    else:
        order = ["mem_k", "mem_v", "q_mem", "k", "q0", "q1", "v", "q2"]
        gives = {"q_mem": [0, 1]} | {f"q{j}": [2 + 2 * j, 3 + 2 * j] for j in range(3)}
        values_of = lambda g: "mem_v" if g < 2 else "v"
        scores_to_turn = 1
    halves = lambda g: [0] if kind == "A" and g >= 2 else [0, 1]
    pieces = [("proj", name, half) for name in order for half in range(2)]
    pieces += [("out", n, t) for n in OUT_ORDER[:2] for t in range(2)]
    last_proj = 2 * len(order) - 1

    steps = []
    to_score, to_turn, to_multiply, to_cat = [], [], [], list(OUT_ORDER)
    finished, done = {}, {}
    to_lo, exped = [], []
    for i, piece in enumerate(pieces + [("end",)]):
        last = piece[0] == "end"
        if not last:
            steps.append(piece)
        if piece == ("proj", "mem_k", 1):
            steps.append(("turn_x", 0))
        if piece == ("proj", "mem_v", 0):
            steps += [("turn_x", 1), ("hi", "mem_k")]
        if i >= last_proj:
            ready = [n for n in to_cat if all(done.get(g, i) < i for g in head_groups(kind, n))][:2]
            steps += [("cat", n) for n in ready]
            to_cat = [n for n in to_cat if n not in ready]
        while to_multiply and finished.get(values_of(to_multiply[0][0]), i) < i and to_multiply[0][2] < i:
            g, c, _ = to_multiply.pop(0)
            steps.append(("values", g, c))
            done[g] = i
        steps += [("probs", g) for g in exped]
        scored = []
        while to_score and (to_score[0][1] < i and not scored or i == last_proj):
            scored.append(to_score.pop(0)[0])
        if i == last_proj:
            scored += gives.get(order[-1], [])
        steps += [("scores", g) for g in scored]
        while to_turn and to_turn[0][1] + scores_to_turn <= i and len(to_multiply) + len(halves(to_turn[0][0])) <= 2:
            g, _ = to_turn.pop(0)
            for c in halves(g):
                steps.append(("turn", g, c))
                to_multiply.append((g, c, i))
        to_turn += [(g, i) for g in scored]
        steps += [("exp", g) for g in scored]
        steps += [("lo", name) for name in to_lo] if last else []
        if not last and piece[2] == 1:
            name = piece[1]
            finished[name] = i
            if i < last_proj:
                to_score += [(g, i) for g in gives.get(name, [])]
            if name != "mem_k":
                steps.append(("hi", name))
        steps += [("lo", name) for name in to_lo] if not last else []
        to_lo = [piece[1]] if not last and piece[2] == 1 else []
        exped = scored
    assert not (to_score or to_turn or to_multiply or to_cat), (to_score, to_turn, to_multiply, to_cat)
    return steps + [("outs", *OUT_ORDER[2:])]


FF_CHUNKS = 22


def plan_ffn():
    units = [("w13", 0), ("w13", 1)]
    for s in range(1, FF_CHUNKS // 2):
        units += [("w13", 2 * s), ("w13", 2 * s + 1), ("w2", s - 1)]
    return units + [("w2", FF_CHUNKS // 2 - 1)]


FFN_HEAD = 5
FFN_TURNS = 4


def build(nc, x_in, mem_in, w13_in, w2_in, ln_g, ln_b, w_mem_kv, w_out, a_w_in, lambdas, subln_g,
          b_w_in, b_sink, out):
    depth, dm, ff2 = w13_in[0].shape
    ff = ff2 // 2
    seq = x_in.shape[1]
    KT = dm // P
    TT = seq // P
    assert (KT, TT, ff) == (8, 2, FF_CHUNKS * P) and depth == 2
    alpha = (2 * depth) ** 0.25

    mixers = [plan_mixer("A"), plan_mixer("B")]
    kinds = ["A", "B"]

    units = []
    ffn_first_unit, mixer_unit = {}, {}
    for layer in range(depth):
        for half in range(2):
            ffn_first_unit[layer, half] = len(units)
            units += [(kind, layer, half, n) for kind, n in plan_ffn()]
            if half == 0:
                for step in mixers[layer]:
                    for name in unit_names(step):
                        mixer_unit[layer, name] = len(units)
                        units.append(("proj" if step[0] == "proj" else "out", layer, name, 0))
    dmas_of = lambda unit: {"w13": 2, "w2": 1, "out": 1}.get(
        unit[0], 4 if unit[1] == 1 and unit[2] in ("q0", "q1", "q2") else
        2 if unit[1] == 0 and str(unit[2]).startswith("qk") else 1)
    landed_at, total = [], [0] * RING
    for n, unit in enumerate(units):
        total[n % RING] += 16 * (dmas_of(unit) - (n == 0))
        landed_at.append(total[n % RING])
    n_units = len(units)
    last_unit = [n for n, unit in enumerate(units) if unit[0] == "w2" and unit[3] == FF_CHUNKS // 2 - 1
                 or unit[0] == "out" and unit[2] == OUT_ORDER[3]]

    proj_of, n_proj = {}, 0
    ffn_first_proj, projections, cat_needs = {}, [], {}
    job_of, n_jobs = {}, 0

    def new_job(key):
        nonlocal n_jobs
        job_of[key] = n_jobs
        n_jobs += 1

    g_turn_of = {}

    def new_g_turn(key):
        nonlocal n_proj
        g_turn_of[key] = (n_proj, len(g_turn_of))
        projections.append(("turning", len(g_turn_of) - 1))
        n_proj += 1

    for t in range(TT):
        for h in range(2):
            new_job(("mem", t, h))
    values_count, n_values = {}, 0
    rms_count, n_rms = {}, 0
    scores_count, n_scores = {}, 0
    biased_count = {}
    q_k_copies, v_copies = {}, {}
    for layer in range(depth):
        for half in range(2):
            ffn_first_proj[layer, half] = n_proj
            n_proj += FF_CHUNKS
            projections += [("chunk", FF_CHUNKS * (2 * layer + half) + f) for f in range(FF_CHUNKS)]
            if half == 0:
                for step in mixers[layer]:
                    if step[0] == "proj" and step[2] == 0:
                        proj_of[layer, step[1]] = n_proj
                        n_proj += 1
                        projections.append(("mixer", (layer, step[1])))
                        if step[1] == "mem_v" or step[1][0] == "v":
                            v_copies[layer, step[1]] = len(v_copies) + 1
                        else:
                            q_k_copies[layer, step[1]] = len(q_k_copies) + 1
                    elif step[0] == "scores":
                        scores_count[layer, step[1]] = n_scores
                        n_scores += 1
                        if step[1] >= 2:
                            biased_count[layer, step[1]] = len(biased_count) + 1
                    elif step[0] == "turn":
                        new_job((layer, *step[1:]))
                        values_count[layer, step[1], step[2]] = n_values
                        n_values += 1
                        if kinds[layer] == "A" and step[1] >= 2:
                            rms_count[layer, step[1]] = n_rms
                            n_rms += 1
                    elif step[0] == "cat":
                        new_g_turn(("cat", layer, step[1]))
                        heads_jobs = [j for key, j in job_of.items() if len(key) == 3 and key[0] == layer
                                      and key[1] in head_groups(kinds[layer], step[1])]
                        cat_needs[layer, step[1]] = [max(j for j in heads_jobs if j % 2 == b)
                                                     for b in range(2) if any(j % 2 == b for j in heads_jobs)]

    ctx = ExitStack()
    with ctx:
        def sb(name, shape, dt=F32):
            return ctx.enter_context(nc.sbuf_tensor(name, shape, dt))

        def sem(name):
            return ctx.enter_context(nc.semaphore(name))

        raw = [sb(f"raw{i}", [P, UNIT]) for i in range(RING)]
        w_hi = [sb(f"w_hi{i}", [P, UNIT], F32R) for i in range(RING)]
        w_lo = [sb(f"w_lo{i}", [P, UNIT], F32R) for i in range(RING)]
        x = sb("x", [P, TT, dm])
        x_t_hi = sb("x_t_hi", [P, KT, seq], F32R)
        x_t_lo = sb("x_t_lo", [P, KT, seq], F32R)
        mem_t_hi = sb("mem_t_hi", [P, KT, seq], F32R)
        mem_t_lo = sb("mem_t_lo", [P, KT, seq], F32R)
        act_hi = sb("act_hi", [P, KT, seq], F32R)
        act_lo = sb("act_lo", [P, KT, seq], F32R)
        wide = sb("wide", [P, TT, dm])
        gain = [sb(f"gain{i}", [P, 2, dm]) for i in range(2)]
        silu = sb("silu", [P, 2, seq])
        gated = sb("gated", [P, 2, seq])
        q_k = sb("q_k", [P, 2, 2, seq])
        k_win = sb("k_win", [P, 2, seq])
        k_mem = sb("k_mem", [P, 2, seq])
        q_mem = sb("q_mem", [P, 2, seq])
        v_tok = sb("v_tok", [P, TT, DIFF_HEADS * P])
        v_mem = sb("v_mem", [P, TT, 4 * HEAD])
        probs = sb("probs", [P, PROBS, 2, TT, seq])
        probs_t = sb("probs_t", [P, 2, TT, seq])
        ident = sb("ident", [P, P])
        minus_dist = sb("minus_dist", [P, TT, seq])
        minus_dist_win = sb("minus_dist_win", [P, TT, seq])
        squares = sb("squares", [P, 2, TT, P])
        bn = sb("bn", [P, 2, 6])
        mean_var = sb("mean_var", [P, TT, 2])
        var_eps = sb("var_eps", [P, TT])
        rstd = sb("rstd", [P, TT])
        z_sum = sb("z_sum", [P, 2])
        shift = sb("shift", [P, 1])
        sq_sum = sb("sq_sum", [P, 2])
        minus_half = sb("minus_half", [P, TT])
        minus_max = sb("minus_max", [P, PROBS, 2, TT])
        sums = sb("sums", [P, PROBS, 2, TT])
        sink_exp = sb("sink_exp", [P, PROBS, 2, TT])
        inv = sb("inv", [P, PROBS, 2, TT])
        rms_sq = sb("rms_sq", [P, 2, TT])
        rms_eps = sb("rms_eps", [P, 2, TT])
        rms = sb("rms", [P, 2, TT])
        sink = sb("sink", [P, WIN_HEADS])
        minus_sink = sb("minus_sink", [P, WIN_HEADS])
        sub_gain = sb("sub_gain", [P, P])
        lam_in = sb("lam_in", [P, 4, HEAD])
        lam_prod = sb("lam_prod", [P, 2, HEAD])
        lam_dot = sb("lam_dot", [P, 2])
        lam_exp = sb("lam_exp", [P, 2])
        minus_lam = sb("minus_lam", [P, 1])

        Y = ctx.enter_context(nc.psum_tensor("Y", [P, TT, dm], F32))
        G = ctx.enter_context(nc.psum_tensor("G", [P, 2, 2, seq], F32))
        T = ctx.enter_context(nc.psum_tensor("T", [P, 2, 512], F32))

        raw_landed = [sem(f"raw_landed{i}") for i in range(RING)]
        hi_made = sem("hi_made")
        lo_made = sem("lo_made")
        unit_used = sem("unit_used")
        silu_made = sem("silu_made")
        gate_steps = sem("gate_steps")
        y_full = sem("y_full")
        turn_full = sem("turn_full")
        turn_copied = sem("turn_copied")
        turn_free = [sem(f"turn_free{i}") for i in range(2)]
        scores_full = sem("scores_full")
        scores_free = sem("scores_free")
        max_made = sem("max_made")
        exp_made = sem("exp_made")
        probs_made = sem("probs_made")
        values_full = sem("values_full")
        squares_made = sem("squares_made")
        rms_made = sem("rms_made")
        g_turn_full = sem("g_turn_full")
        g_turn_hi = sem("g_turn_hi")
        g_turn_lo = sem("g_turn_lo")
        q_k_copied = sem("q_k_copied")
        v_copied = sem("v_copied")
        y_read = sem("y_read")
        var_made = sem("var_made")
        shift_made = sem("shift_made")
        z_squared = sem("z_squared")
        rstd_made = sem("rstd_made")
        x_made = sem("x_made")
        gain_landed = [sem(f"gain_landed{i}") for i in range(2)]
        x_turn_full = sem("x_turn_full")
        x_turn_hi = sem("x_turn_hi")
        x_turn_lo = sem("x_turn_lo")
        x_landed = [sem(f"x_landed{t}") for t in range(TT)]
        gate0_landed = sem("gate0_landed")
        gate0_hi_made = sem("gate0_hi_made")
        first_half_lo_made = sem("first_half_lo_made")
        mem_landed = sem("mem_landed")
        small_landed = sem("small_landed")
        ident_made = sem("ident_made")
        dist_made = sem("dist_made")
        lam_dotted = sem("lam_dotted")
        lam_exped = sem("lam_exped")
        dve_done = sem("dve_done")
        pool_done = sem("pool_done")
        out_landed = sem("out_landed")

        block = ctx.enter_context(nc.Block())

        def at(value, per_turn, turn):
            return value if turn is None else value + turn * per_turn

        FFN_UNIT_STEP = 6

        def last_job_of_count(n):
            group = [key for key, m in scores_count.items() if m == n][0]
            return max(j for key, j in job_of.items() if key[:2] == group)

        def x_turn(n, t, h):
            return 2 * TT * (n + 1) + 2 * t + h

        def first_half(unit):
            return unit[:, :].rearrange("p (k g n) -> p g k n", k=KT, g=2)[:, 0]

        def second_half(unit):
            return unit[:, :].rearrange("p (k g n) -> p g k n", k=KT, g=2)[:, 1]

        def mem_tile_after(layer, half, j):
            return {3: [0], 4: [1]}.get(j, []) if (layer, half) == (0, 0) else []

        @block.sync
        def _(sp):
            def load(u, turn=None):
                kind, layer, which, n = units[u]
                dst = raw[u % RING]
                done = raw_landed[u % RING]
                if u >= RING:
                    sp.wait_ge(lo_made, at(u - RING + 1, FFN_UNIT_STEP, turn))
                if kind == "w13":
                    src = w13_in[which][layer].rearrange("(k p) n -> p k n", p=P)
                    to = dst[:, :].rearrange("p (k g n) -> p g k n", k=KT, g=2)
                    for g in range(2):
                        col = at(g * ff + n * P, 4 * P, turn)
                        sp.dma_start(to[:, g], src[:, :, bass.ds(col, P)])\
                          .then_inc(gate0_landed if (u, g) == (0, 0) else done, 16)
                elif kind in ("w2", "out"):
                    w = w2_in[which][layer] if kind == "w2" else w_out[layer]
                    pair = n if kind == "w2" else which
                    src = w.rearrange("(m p) n -> p m n", p=P)
                    to = dst[:, :].rearrange("p (m n) -> p m n", m=2)
                    sp.dma_start(to, src[:, bass.ds(at(2 * pair, 4, turn), 2), :]).then_inc(done, 16)
                else:
                    name = which
                    if name in ("mem_k", "mem_v"):
                        w, cols = w_mem_kv[layer], [(4 * HEAD if name == "mem_v" else 0, 4 * HEAD)]
                    elif layer == 0:
                        w = a_w_in[0]
                        width = DIFF_HEADS * P
                        if name == "q_mem":
                            cols = [(3 * width, 256)]
                        elif name[0] == "v":
                            cols = [(2 * width + 256 * int(name[1]), 256)]
                        else:
                            cols = [(P * int(name[2]), P), (width + P * int(name[2]), P)]
                    else:
                        w = b_w_in[0]
                        width = WIN_HEADS * HEAD
                        if name == "q_mem":
                            cols = [(width + 512, 256)]
                        elif name == "k":
                            cols = [(width, 256)]
                        elif name == "v":
                            cols = [(width + 256, 256)]
                        else:
                            heads = [h for g in (2 * int(name[1]), 2 * int(name[1]) + 1) for h in window_heads(g)]
                            cols = [(h * HEAD, HEAD) for h in heads]
                    src = w.rearrange("(k p) n -> p k n", p=P)
                    to = dst[:, :].rearrange("p (k n) -> p k n", k=KT)
                    at_col = 0
                    for col, width in cols:
                        sp.dma_start(to[:, :, at_col:at_col + width], src[:, :, col:col + width]).then_inc(done, 16)
                        at_col += width

            for t in range(TT):
                sp.dma_start(x[:, t, :], x_in[0, t * P:(t + 1) * P, :]).then_inc(x_landed[t], 16)
            for layer in range(depth):
                for half in range(2):
                    u0 = ffn_first_unit[layer, half]
                    for j in range(FFN_HEAD):
                        load(u0 + j)
                    with sp.Fori(0, FFN_TURNS) as turn:
                        for j in range(6):
                            load(u0 + FFN_HEAD + j, turn)
                    for j in range(FFN_HEAD + 6 * FFN_TURNS, 33):
                        load(u0 + j)
                    if half == 0:
                        for step in mixers[layer]:
                            for name in unit_names(step):
                                load(mixer_unit[layer, name])
            norm = 3 * depth - 1
            for t in range(TT):
                for h in range(2):
                    sp.wait_ge(x_made, 4 * norm + 2 * t + h + 1)
                    sp.dma_start(out[0, t * P:(t + 1) * P, h * 512:(h + 1) * 512],
                                 x[:, t, h * 512:(h + 1) * 512]).then_inc(out_landed, 16)
            sp.wait_ge(out_landed, 16 * 2 * TT)

        @block.gpsimd
        def _(pool):
            count = [0]

            def link(ins):
                count[0] += 1
                ins.then_inc(pool_done, 1)
                pool.wait_ge(pool_done, count[0])

            link(pool.memset(ident[:, :], 0.0))
            pool.affine_select(out=ident[:, :], in_=ident[:, :], compare_op=ALU.not_equal, fill=1.0,
                               base=0, pattern=[[-1, P]], channel_multiplier=1).then_inc(ident_made, 1)
            pool.iota(minus_dist[:, :, :], [[P, TT], [-1, seq]], base=0, channel_multiplier=1,
                      allow_small_or_imprecise_dtypes=True).then_inc(dist_made, 1)
            link(pool.memset(minus_half[:, :], -0.5))

            def norm_rstd(norm):
                for t in range(TT):
                    if t == 0:
                        pool.wait_ge(z_squared, 2 * norm + 2)
                        link(pool.tensor_scalar(var_eps[:, 0:1], sq_sum[:, 0:1], sq_sum[:, 1:2], LN_EPS / alpha ** 2,
                                                ALU.add, ALU.add))
                    else:
                        pool.wait_ge(var_made, norm + 1)
                    pool.tensor_tensor(rstd[:, t:t + 1], var_eps[:, t:t + 1], minus_half[:, 0:1],
                                       ALU.pow).then_inc(rstd_made, 1)

            for layer in range(depth):
                norm_rstd(3 * layer)
                for step in mixers[layer]:
                    if step[0] == "values" and (layer, step[1]) in rms_count:
                        n = rms_count[layer, step[1]]
                        pool.wait_ge(squares_made, 2 * n + 2)
                        link(pool.tensor_scalar(rms_eps[:, n % 2], rms_sq[:, n % 2], 1.0 / P, LN_EPS,
                                                ALU.mult, ALU.add))
                        pool.tensor_tensor(rms[:, n % 2], rms_eps[:, n % 2], minus_half[:, :],
                                           ALU.pow).then_inc(rms_made, 1)
                norm_rstd(3 * layer + 1)
                norm_rstd(3 * layer + 2)

        @block.scalar
        def _(act):
            def load_gain(norm):
                i, layer = norm % 3, norm // 3
                buf = norm % 2
                for j, src in enumerate((ln_g[i], ln_b[i])):
                    act.dma_start(gain[buf][:, j, :], src[layer:layer + 1, :].to_broadcast([P, dm]))\
                       .then_inc(gain_landed[buf], 16)

            def load_small():
                for i, v in enumerate(lambdas):
                    act.dma_start(lam_in[:, i, :], v[0:1, :].to_broadcast([P, HEAD])).then_inc(small_landed, 16)
                act.dma_start(sub_gain[:, :], subln_g[0:1, :].to_broadcast([P, P])).then_inc(small_landed, 16)
                act.dma_start(sink[:, :], b_sink[0:1, :].to_broadcast([P, WIN_HEADS])).then_inc(small_landed, 16)

            def next_gain(n):
                if n + 2 < 3 * depth:
                    act.wait_ge(x_made, 4 * (n + 1))
                    load_gain(n + 2)

            def split_hi(u, turn=None):
                if u >= n_units:
                    return
                per = 16 * 2 * dmas_of(units[u])
                act.wait_ge(raw_landed[u % RING], at(landed_at[u], per, turn))
                if u >= RING:
                    act.wait_ge(unit_used, at(u - RING + 1, FFN_UNIT_STEP, turn))
                act.activation(w_hi[u % RING][:, :], raw[u % RING][:, :], ACT.Copy).then_inc(hi_made, 1)

            def copy_turned(job, dst):
                act.wait_ge(turn_full, job + 1)
                act.activation(dst, T[:, job % 2, :], ACT.Copy).then_inc(turn_copied, 1)

            def x_hi(n, t):
                for h in range(2):
                    act.wait_ge(x_turn_full, x_turn(n, t, h) + 1)
                    act.activation(x_t_hi[:, 4 * h:4 * h + 4, t * P:(t + 1) * P],
                                   Y[:, t, h * 512:(h + 1) * 512].rearrange("p (a b) -> p a b", a=4),
                                   ACT.Copy).then_inc(x_turn_hi, 1)

            def ffn(layer, half):
                u0, p0 = ffn_first_unit[layer, half], ffn_first_proj[layer, half]
                plan = plan_ffn()

                def after(j, turn=None):
                    kind, n = plan[j]
                    if kind == "w13":
                        p = p0 + n
                        act.wait_ge(unit_used, at(u0 + j + 1, FFN_UNIT_STEP, turn))
                        act.activation(silu[:, p % 2, :], G[:, p % 2, 0, :], ACT.Silu).then_inc(silu_made, 1)
                    split_hi(u0 + j + RING, turn)

                for j in range(FFN_HEAD):
                    after(j)
                    if (layer, half, j) == (0, 0, 1):
                        load_small()
                    if (layer, half) == (0, 0) and j in (2, 3):
                        load_gain(j - 2)
                    for t in mem_tile_after(layer, half, j):
                        for h in range(2):
                            job = job_of["mem", t, h]
                            act.wait_ge(turn_full, job + 1)
                            act.activation(mem_t_hi[:, 4 * h:4 * h + 4, t * P:(t + 1) * P],
                                           T[:, job % 2, :].rearrange("p (a b) -> p a b", a=4),
                                           ACT.Copy).then_inc(turn_copied, 1)
                with act.Fori(0, FFN_TURNS) as turn:
                    for j in range(FFN_HEAD, FFN_HEAD + 6):
                        after(j, turn)
                for j in range(FFN_HEAD + 6 * FFN_TURNS, 31):
                    after(j)

            def norm(n):
                assert dm == 32 * 32
                act.wait_ge(shift_made, n + 1)
                for h in range(2):
                    part = slice(h * 512, (h + 1) * 512)
                    act.activation(Y[:, 0, part], wide[:, 0, part], ACT.Square, bias=shift[:, 0:1],
                                   scale=1.0 / 32, accum_out=sq_sum[:, h:h + 1]).then_inc(z_squared, 1)
                if n < 3 * depth - 1:
                    for t in range(TT):
                        split_hi(last_unit[n] + RING - 1 + t)
                        if n % 3:
                            x_hi(n, t)
                    if n % 3:
                        next_gain(n)

            def mixer(layer):
                if kinds[layer] == "A":
                    act.wait_ge(lam_dotted, 1)
                    act.activation(lam_exp[:, :], lam_dot[:, :], ACT.Exp).then_inc(lam_exped, 1)
                for step in mixers[layer]:
                    if step[0] == "proj" and step[2] == 1:
                        name = step[1]
                        u, p = mixer_unit[layer, name], proj_of[layer, name]
                        act.wait_ge(unit_used, u + 1)
                        if (layer, name) in v_copies:
                            if name == "mem_v":
                                dst = v_mem[:, :, :]
                            elif kinds[layer] == "A":
                                dst = v_tok[:, :, 256 * int(name[1]):256 * int(name[1]) + 256]
                            else:
                                dst = v_tok[:, :, 0:256]
                            act.activation(dst, G[:, p % 2, :, :], ACT.Copy).then_inc(v_copied, 1)
                        else:
                            bank = G[:, p % 2, :, :]
                            scale = HEAD ** -0.5
                            if name == "mem_k":
                                last = act.activation(k_mem[:, :, :], bank, ACT.Copy)
                            elif name == "q_mem":
                                last = act.activation(q_mem[:, :, :], bank, ACT.Copy, scale=scale)
                            elif name == "k":
                                last = act.activation(k_win[:, :, :], bank, ACT.Copy)
                            elif kinds[layer] == "B":
                                j = int(name[1])
                                if j >= 2:
                                    act.wait_ge(scores_full, scores_count[layer, 2 + 2 * (j - 2) + 1] + 1)
                                last = act.activation(q_k[:, j % 2, :, :], bank, ACT.Copy, scale=scale)
                            else:
                                h = int(name[2])
                                if h >= 2:
                                    act.wait_ge(scores_full, scores_count[layer, 2 + h - 2] + 1)
                                act.activation(q_k[:, h % 2, 0, :], bank[:, 0, :], ACT.Copy, scale=scale)
                                last = act.activation(q_k[:, h % 2, 1, :], bank[:, 1, :], ACT.Copy)
                            last.then_inc(q_k_copied, 1)
                    elif step[0] == "turn_x":
                        x_hi(3 * layer, step[1])
                        if step[1] == TT - 1:
                            next_gain(3 * layer)
                    elif step[0] == "hi":
                        split_hi(mixer_unit[layer, step[1]] + RING)
                    elif step[0] == "exp":
                        g = step[1]
                        n = scores_count[layer, g]
                        b = n % PROBS
                        act.wait_ge(max_made, n + 1)
                        if g < 2 and n >= PROBS:
                            act.wait_ge(turn_full, last_job_of_count(n - PROBS) + 1)
                        for c in range(2):
                            for t in range(TT):
                                src = probs[:, b, c, t, :]
                                if g < 2:
                                    src = Y[:, n % 2, (2 * c + t) * seq:(2 * c + t + 1) * seq]
                                last = act.activation(probs[:, b, c, t, :], src, ACT.Exp,
                                                      bias=minus_max[:, b, c, t:t + 1],
                                                      accum_out=sums[:, b, c, t:t + 1])
                            if kinds[layer] == "B" and g >= 2:
                                h = window_heads(g - 2)[c]
                                last = act.activation(sink_exp[:, b, c, :], minus_max[:, b, c, :], ACT.Exp,
                                                      bias=sink[:, h:h + 1])
                        last.then_inc(exp_made, 1)
                    elif step[0] == "turn":
                        job = job_of[layer, step[1], step[2]]
                        n = values_count[layer, step[1], step[2]]
                        copy_turned(job, probs_t[:, n % 2].rearrange("p a b -> p (a b)"))
                    elif step[0] == "values":
                        if (layer, step[1]) in rms_count:
                            n = rms_count[layer, step[1]]
                            job = job_of[layer, step[1], step[2]]
                            act.wait_ge(values_full, values_count[layer, step[1], step[2]] + 1)
                            if n >= 2:
                                act.wait_ge(rms_made, n - 1)
                            for t in range(TT):
                                act.activation(squares[:, n % 2, t, :], T[:, job % 2, t * P:(t + 1) * P], ACT.Square,
                                               accum_out=rms_sq[:, n % 2, t:t + 1]).then_inc(squares_made, 1)
                    elif step[0] == "cat":
                        kp = step[1]
                        p, c = g_turn_of["cat", layer, kp]
                        act.wait_ge(g_turn_full, c + 1)
                        act.activation(act_hi[:, 2 * kp:2 * kp + 2, :], G[:, p % 2, :, :],
                                       ACT.Copy).then_inc(g_turn_hi, 1)

            x_hi(-1, 0)
            act.wait_ge(gate0_landed, 16)
            act.activation(first_half(w_hi[0]), first_half(raw[0]), ACT.Copy).then_inc(gate0_hi_made, 1)
            x_hi(-1, 1)
            act.wait_ge(raw_landed[0], landed_at[0])
            act.activation(second_half(w_hi[0]), second_half(raw[0]), ACT.Copy).then_inc(hi_made, 1)
            for u in range(1, RING):
                split_hi(u)
            for t in range(TT):
                act.dma_start(wide[:, t, :], mem_in[0, t * P:(t + 1) * P, :]).then_inc(mem_landed, 16)
            for layer in range(depth):
                ffn(layer, 0)
                norm(3 * layer)
                mixer(layer)
                norm(3 * layer + 1)
                ffn(layer, 1)
                norm(3 * layer + 2)

        @block.vector
        def _(dve):
            count = [0]

            def link(ins):
                count[0] += 1
                ins.then_inc(dve_done, 1)
                dve.wait_ge(dve_done, count[0])

            def split_lo(u, turn=None):
                if u >= n_units:
                    return
                dve.wait_ge(hi_made, at(u + 1, FFN_UNIT_STEP, turn))
                dve.tensor_tensor(w_lo[u % RING][:, :], raw[u % RING][:, :],
                                  w_hi[u % RING][:, :].bitcast(F32), ALU.subtract).then_inc(lo_made, 1)

            def x_lo(n, order=((0, 0), (1, 0), (0, 1), (1, 1))):
                for t, h in order:
                    part = (slice(None), slice(4 * h, 4 * h + 4), slice(t * P, (t + 1) * P))
                    dve.wait_ge(x_turn_hi, x_turn(n, t, h) + 1)
                    dve.tensor_tensor(x_t_lo[part], Y[:, t, h * 512:(h + 1) * 512].rearrange("p (a b) -> p a b", a=4),
                                      x_t_hi[part].bitcast(F32), ALU.subtract).then_inc(x_turn_lo, 1)

            def ffn(layer, half):
                u0, p0 = ffn_first_unit[layer, half], ffn_first_proj[layer, half]
                chunk0 = FF_CHUNKS * (2 * layer + half)
                plan = plan_ffn()

                def after(j, turn=None):
                    kind, n = plan[j]
                    if kind == "w13":
                        b, slot, c = (p0 + n) % 2, n % 4, chunk0 + n
                        dve.wait_ge(silu_made, at(c + 1, 4, turn))
                        dve.tensor_tensor(gated[:, b, :], silu[:, b, :], G[:, b, 1, :], ALU.mult)\
                           .then_inc(gate_steps, 1)
                        dve.wait_ge(gate_steps, at(3 * c + 1, 12, turn))
                        dve.tensor_copy(act_hi[:, slot, :], gated[:, b, :]).then_inc(gate_steps, 1)
                        dve.wait_ge(gate_steps, at(3 * c + 2, 12, turn))
                        dve.tensor_tensor(act_lo[:, slot, :], gated[:, b, :], act_hi[:, slot, :].bitcast(F32),
                                          ALU.subtract).then_inc(gate_steps, 1)
                    split_lo(u0 + j + RING, turn)

                for j in range(FFN_HEAD):
                    after(j)
                    for t in mem_tile_after(layer, half, j):
                        for h in range(2):
                            part = (slice(None), slice(4 * h, 4 * h + 4), slice(t * P, (t + 1) * P))
                            job = job_of["mem", t, h]
                            dve.wait_ge(turn_copied, job + 1)
                            dve.tensor_tensor(mem_t_lo[part], T[:, job % 2, :].rearrange("p (a b) -> p a b", a=4),
                                              mem_t_hi[part].bitcast(F32), ALU.subtract)\
                               .then_inc(turn_free[job % 2], 1)
                with dve.Fori(0, FFN_TURNS) as turn:
                    for j in range(FFN_HEAD, FFN_HEAD + 6):
                        after(j, turn)
                for j in range(FFN_HEAD + 6 * FFN_TURNS, 31):
                    after(j)

            def norm(n):
                c = (1.0 if n % 3 == 1 else 0.5) / alpha
                g = gain[n % 2]
                dve.wait_ge(gain_landed[n % 2], 32 * (n // 2 + 1))
                halves = [slice(h * 512, (h + 1) * 512) for h in range(2)]

                def take(t, h, accum=None):
                    if (t, h) == (TT - 1, 1):
                        dve.wait_ge(unit_used, last_unit[n] + 1)
                    else:
                        dve.wait_ge(y_full, (2 * TT - 1) * n + 2 * t + h + 1)
                    part = halves[h]
                    dve.scalar_tensor_tensor(out=wide[:, t, part], in0=Y[:, t, part], scalar=c, in1=x[:, t, part],
                                             op0=ALU.mult, op1=ALU.add, accum_out=accum).then_inc(y_read, 1)
                    return 2 * (TT * n + t) + h + 1

                def times_gain(t, h):
                    part = halves[h]
                    count[0] += 1
                    dve.scalar_tensor_tensor(out=x[:, t, part], in0=wide[:, t, part], scalar=mean_var[:, t, 0:1],
                                             in1=g[:, 0, part], op0=ALU.subtract, op1=ALU.mult).then_inc(dve_done, 1)
                    return count[0]

                def plus_bias(t, h, made):
                    part = halves[h]
                    dve.wait_ge(dve_done, made)
                    dve.scalar_tensor_tensor(out=x[:, t, part], in0=x[:, t, part], scalar=rstd[:, t:t + 1],
                                             in1=g[:, 1, part], op0=ALU.mult, op1=ALU.add).then_inc(x_made, 1)

                for h in range(2):
                    taken = take(0, h, z_sum[:, h:h + 1])
                dve.wait_ge(y_read, taken)
                dve.tensor_scalar(shift[:, :], z_sum[:, 0:1], z_sum[:, 1:2], -1.0 / (32 * dm), ALU.add, ALU.mult)\
                   .then_inc(shift_made, 1)
                link(dve.tensor_scalar(mean_var[:, 0, 0:1], z_sum[:, 0:1], z_sum[:, 1:2], 1.0 / dm, ALU.add, ALU.mult))
                made = [times_gain(0, h) for h in range(2)]
                dve.wait_ge(y_read, take(1, 0))
                dve.bn_stats(bn[:, 0, :], wide[:, 1, halves[0]])
                dve.wait_ge(rstd_made, TT * n + 1)
                for h in range(2):
                    plus_bias(0, h, made[h])
                if n % 3 == 0:
                    split_lo(last_unit[n] + RING - 1)
                dve.wait_ge(y_read, take(1, 1))
                link(dve.bn_stats(bn[:, 1, :], wide[:, 1, halves[1]]))
                link(dve.bn_aggr(mean_var[:, 1, :], bn[:, :, :].rearrange("p a b -> p (a b)")))
                dve.tensor_scalar(var_eps[:, 1:2], mean_var[:, 1, 1:2], LN_EPS / alpha ** 2, None,
                                  ALU.add).then_inc(var_made, 1)
                if n == 3 * depth - 1:
                    made = [times_gain(1, h) for h in range(2)]
                    dve.wait_ge(rstd_made, TT * n + 2)
                    for h in range(2):
                        plus_bias(1, h, made[h])
                    return
                made = times_gain(1, 0)
                dve.wait_ge(rstd_made, TT * n + 2)
                plus_bias(1, 0, made)
                plus_bias(1, 1, times_gain(1, 1))
                x_lo(n)
                if n % 3:
                    split_lo(last_unit[n] + RING - 1)
                    split_lo(last_unit[n] + RING)
                else:
                    u = last_unit[n] + RING
                    dve.wait_ge(hi_made, u + 1)
                    for of, done in ((first_half, first_half_lo_made), (second_half, lo_made)):
                        dve.tensor_tensor(of(w_lo[u % RING]), of(raw[u % RING]), of(w_hi[u % RING]).bitcast(F32),
                                          ALU.subtract).then_inc(done, 1)

            def small_parameters():
                dve.wait_ge(small_landed, 16 * 6)
                for i in range(2):
                    last = dve.tensor_tensor(lam_prod[:, i, :], lam_in[:, 2 * i, :], lam_in[:, 2 * i + 1, :], ALU.mult)
                link(last)
                dve.tensor_reduce(lam_dot[:, :], lam_prod[:, :, :], AX_X, ALU.add).then_inc(lam_dotted, 1)
                dve.tensor_scalar(minus_sink[:, :], sink[:, :], -1.0, None, ALU.mult)
                link(dve.tensor_scalar(sub_gain[:, :], sub_gain[:, :], 1.0 - LAM_INIT, None, ALU.mult))

            def mixer(layer):
                a = kinds[layer] == "A"
                if a:
                    dve.wait_ge(lam_exped, 1)
                    link(dve.tensor_tensor(minus_lam[:, :], lam_exp[:, 1:2], lam_exp[:, 0:1], ALU.subtract))
                    link(dve.tensor_scalar(minus_lam[:, :], minus_lam[:, :], -LAM_INIT, None, ALU.add))
                for step in mixers[layer]:
                    if step[0] == "lo":
                        split_lo(mixer_unit[layer, step[1]] + RING)
                    elif step[0] == "scores":
                        g = step[1]
                        n = scores_count[layer, g]
                        b = n % PROBS
                        flat = minus_max[:, b].rearrange("p c t -> p (c t)")
                        dve.wait_ge(scores_full, n + 1)
                        if g < 2:
                            dve.tensor_reduce(flat, Y[:, n % 2, :].rearrange("p (m k) -> p m k", m=4), AX_X,
                                              ALU.max, negate=True).then_inc(max_made, 1)
                            continue
                        if n >= PROBS:
                            dve.wait_ge(turn_full, last_job_of_count(n - PROBS) + 1)
                        for c in range(2):
                            src = Y[:, n % 2, c * 512:(c + 1) * 512]
                            dst = probs[:, b, c].rearrange("p a b -> p (a b)")
                            s = slope(DIFF_HEADS, g - 2) if a else slope(WIN_HEADS, window_heads(g - 2)[c])
                            dist = (minus_dist if a else minus_dist_win)[:, :, :]
                            last = dve.scalar_tensor_tensor(
                                out=dst, in0=dist.rearrange("p a b -> p (a b)"), scalar=s, in1=src,
                                op0=ALU.mult, op1=ALU.add)
                        last.then_inc(scores_free, 1)
                        dve.wait_ge(scores_free, biased_count[layer, g])
                        top = dve.tensor_reduce(flat, probs[:, b].rearrange("p c t k -> p (c t) k"), AX_X,
                                                ALU.max, negate=True)
                        if not a:
                            link(top)
                            for c in range(2):
                                h = window_heads(g - 2)[c]
                                top = dve.tensor_scalar(minus_max[:, b, c, :], minus_max[:, b, c, :],
                                                        minus_sink[:, h:h + 1], None, ALU.min)
                        top.then_inc(max_made, 1)
                    elif step[0] == "probs":
                        g = step[1]
                        n = scores_count[layer, g]
                        b = n % PROBS
                        dve.wait_ge(exp_made, n + 1)
                        flat = lambda s: s[:, b].rearrange("p c t -> p (c t)")
                        if not a and g >= 2:
                            link(dve.tensor_tensor(flat(sums), flat(sums), flat(sink_exp), ALU.add))
                        if not a or g < 2:
                            dve.reciprocal(flat(inv), flat(sums)).then_inc(probs_made, 1)
                            continue
                        link(dve.reciprocal(flat(inv), flat(sums)))
                        link(dve.tensor_scalar(inv[:, b, 1, :], inv[:, b, 1, :], minus_lam[:, 0:1], None, ALU.mult))
                        for t in range(TT):
                            last = dve.tensor_scalar(probs[:, b, 1, t, :], probs[:, b, 1, t, :],
                                                     inv[:, b, 1, t:t + 1], None, ALU.mult)
                        link(last)
                        for t in range(TT):
                            last = dve.scalar_tensor_tensor(
                                out=probs[:, b, 0, t, :], in0=probs[:, b, 0, t, :], scalar=inv[:, b, 0, t:t + 1],
                                in1=probs[:, b, 1, t, :], op0=ALU.mult, op1=ALU.add)
                        last.then_inc(probs_made, 1)
                    elif step[0] == "values":
                        g, c = step[1:]
                        job, n = job_of[layer, g, c], values_count[layer, g, c]
                        b = scores_count[layer, g] % PROBS
                        bank = T[:, job % 2, :]
                        if (layer, g) in rms_count:
                            r = rms_count[layer, g]
                            dve.wait_ge(rms_made, r + 1)
                            col = (g - 2) * P
                            for t in range(TT):
                                last = dve.scalar_tensor_tensor(
                                    out=wide[:, t, col:col + P], in0=bank[:, t * P:(t + 1) * P],
                                    scalar=rms[:, r % 2, t:t + 1], in1=sub_gain[:, :], op0=ALU.mult, op1=ALU.mult)
                        else:
                            dve.wait_ge(values_full, n + 1)
                            head = WIN_HEADS + 2 * g + c if g < 2 else window_heads(g - 2)[c]
                            for t in range(TT):
                                last = dve.tensor_scalar(
                                    wide[:, t, head * HEAD:(head + 1) * HEAD], bank[:, t * HEAD:(t + 1) * HEAD],
                                    inv[:, b, c, t:t + 1], None, ALU.mult)
                        last.then_inc(turn_free[job % 2], 1)
                    elif step[0] == "cat":
                        kp = step[1]
                        p, c = g_turn_of["cat", layer, kp]
                        dve.wait_ge(g_turn_hi, c + 1)
                        dve.tensor_tensor(act_lo[:, 2 * kp:2 * kp + 2, :], G[:, p % 2, :, :],
                                          act_hi[:, 2 * kp:2 * kp + 2, :].bitcast(F32),
                                          ALU.subtract).then_inc(g_turn_lo, 1)

            dve.wait_ge(dist_made, 1)
            flat = lambda s: s[:, :, :].rearrange("p a b -> p (a b)")
            link(dve.scalar_tensor_tensor(out=flat(minus_dist), in0=flat(minus_dist), scalar=-1.0,
                                          in1=flat(minus_dist), op0=ALU.mult, op1=ALU.min))
            link(dve.tensor_scalar(flat(minus_dist_win), flat(minus_dist), -float(WINDOW), NEG,
                                   ALU.is_lt, ALU.mult))
            link(dve.tensor_tensor(flat(minus_dist_win), flat(minus_dist_win), flat(minus_dist), ALU.add))
            x_lo(-1, ((0, 0), (0, 1)))
            dve.wait_ge(gate0_hi_made, 1)
            dve.tensor_tensor(first_half(w_lo[0]), first_half(raw[0]), first_half(w_hi[0]).bitcast(F32),
                              ALU.subtract).then_inc(first_half_lo_made, 1)
            x_lo(-1, ((1, 0), (1, 1)))
            dve.wait_ge(hi_made, 1)
            dve.tensor_tensor(second_half(w_lo[0]), second_half(raw[0]), second_half(w_hi[0]).bitcast(F32),
                              ALU.subtract).then_inc(lo_made, 1)
            for u in range(1, RING):
                split_lo(u)
            for layer in range(depth):
                ffn(layer, 0)
                if layer == 0:
                    small_parameters()
                norm(3 * layer)
                mixer(layer)
                norm(3 * layer + 1)
                ffn(layer, 1)
                norm(3 * layer + 2)

        @block.tensor
        def _(pe):
            PASSES = [(0, 0), (0, 1), (1, 0)]

            def job_done(job):
                pe.wait_ge(turn_free[job % 2], job // 2 + 1)

            def start_job(job):
                if job >= 2:
                    job_done(job - 2)

            def turn_x(n, t):
                if t == TT - 1 and n >= 0 and n % 3:
                    for _ in range(KEEP_BUSY):
                        pe.matmul(T[:, 0, 0:seq], act_hi[:, 0, 0:P], act_hi[:, 0, :], start=True, stop=True)
                for h in range(2):
                    if n >= 0:
                        pe.wait_ge(x_made, 4 * n + 2 * t + h + 1)
                    for k in range(4 * h, 4 * h + 4):
                        last = pe.transpose(Y[:, t, k * P:(k + 1) * P], x[:, t, k * P:(k + 1) * P], ident[:, :])
                    last.then_inc(x_turn_full, 1)

            def turn_mem(t):
                for h in range(2):
                    job = job_of["mem", t, h]
                    start_job(job)
                    for k in range(4):
                        col = (4 * h + k) * P
                        last = pe.transpose(T[:, job % 2, k * P:(k + 1) * P], wide[:, t, col:col + P], ident[:, :])
                    last.then_inc(turn_full, 1)

            def x_turned(n, h):
                pe.wait_ge(x_turn_lo, 2 * TT * (n + 1) + (TT + h + 1 if n < 0 else TT * (h + 1)))

            def wait_weights(u, turn=None):
                pe.wait_ge(lo_made, at(u + 1, FFN_UNIT_STEP, turn))

            def feature_major(u, p, src_hi, src_lo, parts=(0, 1), norm=None):
                moving = (src_hi, src_lo)
                view = [w[u % RING][:, :].rearrange("p (k g n) -> p k g n", k=KT, g=2) for w in (w_hi, w_lo)]
                for g in parts:
                    for k in range(KT):
                        if norm is not None and g == 0 and k % 4 == 0:
                            x_turned(norm, k // 4)
                        for i, (wi, xi) in enumerate(PASSES):
                            last = pe.matmul(G[:, p % 2, g, :], view[wi][:, k, g, :], moving[xi][:, k, :],
                                             start=(k == 0 and i == 0), stop=(k == KT - 1 and i == 2))
                if 1 in parts:
                    last.then_inc(unit_used, 1)

            def token_major(u, p, src_hi, src_lo, parts):
                stationary = (src_hi, src_lo)
                view = [w[u % RING][:, :].rearrange("p (k n) -> p k n", k=KT) for w in (w_hi, w_lo)]
                for t in parts:
                    for k in range(KT):
                        for i, (wi, xi) in enumerate(PASSES):
                            last = pe.matmul(G[:, p % 2, t, :], stationary[xi][:, k, t * P:(t + 1) * P],
                                             view[wi][:, k, :], start=(k == 0 and i == 0),
                                             stop=(k == KT - 1 and i == 2))
                if 1 in parts:
                    last.then_inc(unit_used, 1)

            def accumulate(u, slots, t, first=False, halves=(0, 1), stop=False):
                view = [w[u % RING][:, :].rearrange("p (m n) -> p m n", m=2) for w in (w_hi, w_lo)]
                stationary = (act_hi, act_lo)
                for half in halves:
                    cols = slice(half * 512, (half + 1) * 512)
                    for m in range(2):
                        for i, (wi, xi) in enumerate(PASSES):
                            last = pe.matmul(Y[:, t, cols], stationary[xi][:, slots[m], t * P:(t + 1) * P],
                                             view[wi][:, m, cols], start=(first and m == 0 and i == 0),
                                             stop=(stop and m == 1 and i == 2))
                return last

            def accumulate_last(parts):
                for t in range(TT):
                    order = [(0, 0), (0, 1), (1, 0), (1, 1)] if t == 0 else [(0, 0), (1, 0), (0, 1), (1, 1)]
                    for n, half in order:
                        u, slots, wait = parts[n]
                        if (t, half) == (0, 0):
                            wait()
                        last = accumulate(u, slots, t, halves=(half,), stop=n == 1)
                        if (t, half) == (TT - 1, 1):
                            last.then_inc(unit_used, 1)
                        elif n == 1:
                            last.then_inc(y_full, 1)

            def scores_read(layer, n):
                g = [g for (l, g), m in scores_count.items() if m == n][0]
                if g < 2:
                    pe.wait_ge(exp_made, n + 1)
                else:
                    pe.wait_ge(scores_free, biased_count[layer, g])

            def bank_free(p, turn=None):
                if p < 2:
                    return
                stage, which = projections[p - 2]
                if stage == "chunk":
                    pe.wait_ge(gate_steps, at(3 * which + 1, 12, turn))
                elif stage == "turning":
                    pe.wait_ge(g_turn_lo, which + 1)
                elif which in q_k_copies:
                    pe.wait_ge(q_k_copied, q_k_copies[which])
                else:
                    pe.wait_ge(v_copied, v_copies[which])

            def ffn(layer, half):
                u0, p0 = ffn_first_unit[layer, half], ffn_first_proj[layer, half]
                chunk0 = FF_CHUNKS * (2 * layer + half)
                plan = plan_ffn()

                def unit(j, turn=None):
                    kind, n = plan[j]
                    u = u0 + j
                    norm = 3 * layer + 2 * half - 1 if j == 0 else None
                    if u == 0:
                        pe.wait_ge(first_half_lo_made, 1)
                        bank_free(p0)
                        feature_major(u, p0, x_t_hi, x_t_lo, (0,), norm)
                        wait_weights(u)
                        feature_major(u, p0, x_t_hi, x_t_lo, (1,))
                        return
                    wait_weights(u, turn)
                    if kind == "w13":
                        bank_free(p0 + n, turn)
                        feature_major(u, p0 + n, x_t_hi, x_t_lo, norm=norm)
                    else:
                        pe.wait_ge(gate_steps, at(3 * (chunk0 + 2 * n + 2), 12, turn))
                        slots = [(2 * n) % 4, (2 * n + 1) % 4]
                        for t in range(TT):
                            last = accumulate(u, slots, t, first=(turn is None and n == 0))
                        last.then_inc(unit_used, 1)

                for j in range(FFN_HEAD):
                    unit(j)
                    for t in mem_tile_after(layer, half, j):
                        pe.wait_ge(mem_landed, 16 * TT)
                        turn_mem(t)
                with pe.Fori(0, FFN_TURNS) as turn:
                    for j in range(FFN_HEAD, FFN_HEAD + 6):
                        unit(j, turn)
                j = FFN_HEAD + 6 * FFN_TURNS
                unit(j)
                unit(j + 1)

                def wait_unit(k):
                    wait_weights(u0 + j + k)
                    pe.wait_ge(gate_steps, 3 * (chunk0 + FF_CHUNKS - (2 if k == 2 else 0)))

                accumulate_last([(u0 + j + 2, [(FF_CHUNKS - 4) % 4, (FF_CHUNKS - 3) % 4], partial(wait_unit, 2)),
                                 (u0 + j + 3, [(FF_CHUNKS - 2) % 4, (FF_CHUNKS - 1) % 4], partial(wait_unit, 3))])

            def mixer(layer):
                a = kinds[layer] == "A"
                norm = 3 * layer
                for step in mixers[layer]:
                    if step[0] == "proj":
                        _, name, half = step
                        u, p = mixer_unit[layer, name], proj_of[layer, name]
                        if half == 0:
                            if name == "q_mem":
                                pe.wait_ge(first_half_lo_made, layer + 2)
                            else:
                                wait_weights(u)
                            bank_free(p)
                        elif name == "q_mem":
                            wait_weights(u)
                        if name == "mem_k":
                            feature_major(u, p, mem_t_hi, mem_t_lo, (half,))
                        elif name == "mem_v":
                            token_major(u, p, mem_t_hi, mem_t_lo, (half,))
                        elif name[0] == "v":
                            token_major(u, p, x_t_hi, x_t_lo, (half,))
                        else:
                            feature_major(u, p, x_t_hi, x_t_lo, (half,), norm if name == "q_mem" else None)
                    elif step[0] == "turn_x":
                        turn_x(norm, step[1])
                    elif step[0] == "scores":
                        g = step[1]
                        n = scores_count[layer, g]
                        b = n % 2
                        if g < 2:
                            pe.wait_ge(q_k_copied, q_k_copies[layer, "q_mem"])
                            q, k = q_mem[:, g, :], k_mem[:, g, :]
                        elif a:
                            pe.wait_ge(q_k_copied, q_k_copies[layer, f"qk{g - 2}"])
                            q, k = q_k[:, g % 2, 0, :], q_k[:, g % 2, 1, :]
                        else:
                            j = (g - 2) // 2
                            pe.wait_ge(q_k_copied, q_k_copies[layer, f"q{j}"])
                            q, k = q_k[:, j % 2, g % 2, :], k_win[:, (g - 2) // 3, :]
                        if g >= 2:
                            scores_read(layer, n - 2)
                        for t in range(TT):
                            for c in range(2):
                                rows = slice(c * HEAD, (c + 1) * HEAD)
                                last = pe.matmul(Y[:, b, c * 512 + t * seq:c * 512 + (t + 1) * seq],
                                                 q[rows, t * P:(t + 1) * P], k[rows, :], start=True, stop=True)
                        last.then_inc(scores_full, 1)
                    elif step[0] == "turn":
                        g, c = step[1:]
                        job = job_of[layer, g, c]
                        n = scores_count[layer, g]
                        pe.wait_ge(probs_made, n + 1)
                        start_job(job)
                        for kt in range(TT):
                            for t in range(TT):
                                at_col = kt * seq + t * P
                                last = pe.transpose(T[:, job % 2, at_col:at_col + P],
                                                    probs[:, n % PROBS, c, t, kt * P:(kt + 1) * P], ident[:, :])
                        last.then_inc(turn_full, 1)
                    elif step[0] == "values":
                        g, c = step[1:]
                        job, n = job_of[layer, g, c], values_count[layer, g, c]
                        pe.wait_ge(turn_copied, job + 1)
                        if g < 2:
                            pe.wait_ge(v_copied, v_copies[layer, "mem_v"])
                            v, width = v_mem[:, :, (2 * g + c) * HEAD:(2 * g + c + 1) * HEAD], HEAD
                        elif a:
                            h = g - 2
                            pe.wait_ge(v_copied, v_copies[layer, f"v{h // 2}"])
                            v, width = v_tok[:, :, h * P:(h + 1) * P], P
                        else:
                            kv = window_heads(g - 2)[c] // WIN_GROUP
                            pe.wait_ge(v_copied, v_copies[layer, "v"])
                            v, width = v_tok[:, :, kv * HEAD:(kv + 1) * HEAD], HEAD
                        for t in range(TT):
                            for kt in range(TT):
                                last = pe.matmul(T[:, job % 2, t * width:(t + 1) * width],
                                                 probs_t[:, n % 2, kt, t * P:(t + 1) * P], v[:, kt, :],
                                                 start=(kt == 0), stop=(kt == TT - 1))
                        last.then_inc(values_full, 1)
                    elif step[0] == "cat":
                        kp = step[1]
                        p, _ = g_turn_of["cat", layer, kp]
                        for job_before in cat_needs[layer, kp]:
                            job_done(job_before)
                        bank_free(p)
                        for m in range(2):
                            for t in range(TT):
                                col = (2 * kp + m) * P
                                last = pe.transpose(G[:, p % 2, m, t * P:(t + 1) * P],
                                                    wide[:, t, col:col + P], ident[:, :])
                        last.then_inc(g_turn_full, 1)
                    elif step[0] == "out":
                        _, kp, t = step
                        u = mixer_unit[layer, kp]
                        first = kp == OUT_ORDER[0]
                        if t == 0:
                            wait_weights(u)
                            pe.wait_ge(g_turn_lo, g_turn_of["cat", layer, kp][1] + 1)
                        if first:
                            scores_read(layer, max(m for (l, _), m in scores_count.items()
                                                   if l == layer and m % 2 == t))
                        last = accumulate(u, [2 * kp, 2 * kp + 1], t, first)
                        if t == 1:
                            last.then_inc(unit_used, 1)
                    elif step[0] == "outs":

                        def wait_unit(kp):
                            wait_weights(mixer_unit[layer, kp])
                            pe.wait_ge(g_turn_lo, g_turn_of["cat", layer, kp][1] + 1)

                        accumulate_last([(mixer_unit[layer, kp], [2 * kp, 2 * kp + 1], partial(wait_unit, kp))
                                         for kp in step[1:]])

            pe.wait_ge(ident_made, 1)
            for t in range(TT):
                pe.wait_ge(x_landed[t], 16)
                turn_x(-1, t)
            for layer in range(depth):
                ffn(layer, 0)
                mixer(layer)
                for t in range(TT):
                    turn_x(3 * layer + 1, t)
                ffn(layer, 1)
                if layer < depth - 1:
                    for t in range(TT):
                        turn_x(3 * layer + 2, t)


def window_heads(g):
    first = g % 3 + 6 * (g // 3)
    return first, first + WIN_GROUP


_INS = ["x", "mem", "ffn1_w13", "ffn1_w2", "ln1_g", "ln1_b", "w_mem_kv", "w_out", "ln2_g", "ln2_b",
        "ffn2_w13", "ffn2_w2", "ln3_g", "ln3_b", "a_w_in", "a_lambda_q1", "a_lambda_k1", "a_lambda_q2",
        "a_lambda_k2", "a_subln_g", "b_w_in", "b_sink"]


def kernel(**inputs):
    import numpy as _np
    import concourse.bacc as _bacc
    from concourse.bass_utils import run_bass_kernel_spmd as _run

    nc = _bacc.Bacc("TRN2", target_bir_lowering=False, num_devices=1)
    arrays, a = {}, {}
    for name in _INS:
        v = _np.ascontiguousarray(inputs[name])
        arrays[f"in_{name}"] = v
        a[name] = nc.dram_tensor(f"in_{name}", v.shape, mybir.dt.from_np(v.dtype), kind="ExternalInput").ap()
    out = nc.dram_tensor("out", arrays["in_x"].shape, F32, kind="ExternalOutput").ap()
    build(nc, a["x"], a["mem"], [a["ffn1_w13"], a["ffn2_w13"]], [a["ffn1_w2"], a["ffn2_w2"]],
          [a["ln1_g"], a["ln2_g"], a["ln3_g"]], [a["ln1_b"], a["ln2_b"], a["ln3_b"]], a["w_mem_kv"],
          a["w_out"], a["a_w_in"], [a["a_lambda_q1"], a["a_lambda_k1"], a["a_lambda_q2"], a["a_lambda_k2"]],
          a["a_subln_g"], a["b_w_in"], a["b_sink"], out)
    r = _run(nc, [arrays], core_ids=[0])
    return r.results[0]["out"]
```
